# Optimizing a Trainium2 kernel written in Bass

```python
import jax, jax.numpy as jnp
from jax import lax
import numpy as np

D_MODEL = 1024
BATCH = 1
SEQ = 1024
DEPTH = 1
DEC_BATCH = 8
DEC_SEQ = 4
PAST_LEN = 2048
PAGE_SIZE = 128

HEAD_DIM = 64
N_ATTN_HEADS = 8
ATTN_WIDTH = N_ATTN_HEADS * HEAD_DIM
CONV_CH = D_MODEL - ATTN_WIDTH
IN_COLS = 3 * ATTN_WIDTH + 2 * CONV_CH
CONV_KERNEL = 31
DIL_CONFIGS = ((128, 1), (512, 4), (2048, 16))
MAX_WINDOW = 2048
KEYS_PER_BRANCH = 128
N_MEM = 256
N_XHEADS = 4
XHEAD_DIM = D_MODEL // N_XHEADS
D_FF = 2816
FFN_CONV = 3
EPS = 1e-6

kernel_name = "hymba_conformer_dilated_swa_decoder_step"

def rms_norm(x, g):
    xf = x.astype(jnp.float32)
    y = xf * lax.rsqrt(jnp.mean(xf * xf, axis=-1, keepdims=True) + EPS)
    return (y * g.astype(jnp.float32)).astype(x.dtype)

def layer_norm(x, g, b):
    xf = x.astype(jnp.float32)
    mu = jnp.mean(xf, axis=-1, keepdims=True)
    var = jnp.mean(jnp.square(xf - mu), axis=-1, keepdims=True)
    y = (xf - mu) * lax.rsqrt(var + EPS) * g.astype(jnp.float32) + b.astype(jnp.float32)
    return y.astype(x.dtype)

def causal_dwconv(x_ctx, w):
    return lax.conv_general_dilated(x_ctx, w[:, None, :], window_strides=(1,), padding="VALID",
                                    dimension_numbers=("NWC", "WIO", "NWC"),
                                    feature_group_count=x_ctx.shape[-1])

def dilated_branch_prompt(q, k, v, dil):
    B, S, H, Dh = q.shape
    blk = KEYS_PER_BRANCH
    span = dil * blk
    sp = -(-S // span) * span
    nb = sp // span
    pad = ((0, 0), (0, sp - S), (0, 0), (0, 0))

    def to_blocks(t):
        return jnp.pad(t, pad).reshape(B, nb, blk, dil, H, Dh)

    def with_prev(t):
        prev = jnp.concatenate([jnp.zeros_like(t[:, :1]), t[:, :-1]], axis=1)
        return jnp.concatenate([prev, t], axis=2)

    qb = to_blocks(q)
    kk = with_prev(to_blocks(k))
    vv = with_prev(to_blocks(v))
    s = jnp.einsum("bnqrhd,bnkrhd->bnrhqk", qb, kk).astype(jnp.float32) * (HEAD_DIM ** -0.5)
    lq = jnp.arange(blk)[:, None]
    lk = jnp.arange(2 * blk)[None, :]
    band = (lk >= lq) & (lk <= lq + blk)
    not_first = (jnp.arange(nb)[:, None, None] > 0) | (lk >= blk)[None]
    mask = band[None] & not_first
    s = jnp.where(mask[None, :, None, None], s, -jnp.inf)
    m = jnp.max(s, axis=-1, keepdims=True)
    p = jnp.exp(s - m)
    den = jnp.sum(p, axis=-1, keepdims=True)
    o = jnp.einsum("bnrhqk,bnkrhd->bnqrhd", (p / den).astype(v.dtype), vv)
    lse = (m + jnp.log(den))[..., 0]
    o = o.reshape(B, sp, H, Dh)[:, :S]
    lse = jnp.transpose(lse, (0, 1, 4, 2, 3)).reshape(B, sp, H)[:, :S]
    return o, lse

def dilated_branch_sample(q, kc, vc, dil):
    T = q.shape[1]
    wb = kc.shape[1] - T
    j = jnp.arange(KEYS_PER_BRANCH + 1)
    idx = wb + jnp.arange(T)[:, None] - dil * j[None, :]
    valid = idx >= 0
    idxc = jnp.maximum(idx, 0)
    kg = kc[:, idxc]
    vg = vc[:, idxc]
    s = jnp.einsum("bthd,btjhd->bthj", q, kg).astype(jnp.float32) * (HEAD_DIM ** -0.5)
    s = jnp.where(valid[None, :, None, :], s, -jnp.inf)
    m = jnp.max(s, axis=-1, keepdims=True)
    p = jnp.exp(s - m)
    den = jnp.sum(p, axis=-1, keepdims=True)
    o = jnp.einsum("bthj,btjhd->bthd", (p / den).astype(vc.dtype), vg)
    lse = (m + jnp.log(den))[..., 0]
    return o, lse

def combine_branches(outs, lses):
    w = jax.nn.softmax(jnp.stack(lses, axis=0), axis=0)
    o = jnp.stack(outs, axis=0)
    return jnp.einsum("gbth,gbthd->bthd", w.astype(o.dtype), o)

def memory_kv(mem, p):
    Bm, M, _ = mem.shape
    mn = rms_norm(mem, p["g_mem"])
    mk = (mn @ p["w_mk"]).reshape(Bm, M, N_XHEADS, XHEAD_DIM)
    mv = (mn @ p["w_mv"]).reshape(Bm, M, N_XHEADS, XHEAD_DIM)
    return mk, mv

def trunk_layer(x, is_prompt, win_k, win_v, conv_ctx, ffn_ctx, mem_k, mem_v, p):
    B, T, _ = x.shape
    h = rms_norm(x, p["g_pre_mix"])
    z = h @ p["w_in"]
    q, k, v, a, gate = jnp.split(z, [ATTN_WIDTH, 2 * ATTN_WIDTH, 3 * ATTN_WIDTH,
                                     3 * ATTN_WIDTH + CONV_CH], axis=-1)
    q = q.reshape(B, T, N_ATTN_HEADS, HEAD_DIM)
    k = k.reshape(B, T, N_ATTN_HEADS, HEAD_DIM)
    v = v.reshape(B, T, N_ATTN_HEADS, HEAD_DIM)
    outs, lses = [], []
    if is_prompt:
        for _, dil in DIL_CONFIGS:
            o_i, l_i = dilated_branch_prompt(q, k, v, dil)
            outs.append(o_i)
            lses.append(l_i)
        wb = min(MAX_WINDOW, T)
        new_k, new_v = k[:, T - wb:], v[:, T - wb:]
    else:
        kc = jnp.concatenate([win_k, k], axis=1)
        vc = jnp.concatenate([win_v, v], axis=1)
        for _, dil in DIL_CONFIGS:
            o_i, l_i = dilated_branch_sample(q, kc, vc, dil)
            outs.append(o_i)
            lses.append(l_i)
        new_k, new_v = k, v
    attn = combine_branches(outs, lses).reshape(B, T, ATTN_WIDTH)
    u = a * jax.nn.sigmoid(gate)
    u_ctx = jnp.concatenate([conv_ctx, u], axis=1)
    c = causal_dwconv(u_ctx, p["conv_w"]) + p["conv_b"]
    c = jax.nn.silu(layer_norm(c, p["ln_conv_g"], p["ln_conv_b"]))
    new_conv = u_ctx[:, -(CONV_KERNEL - 1):]
    mix = jnp.concatenate([rms_norm(attn, p["g_out_attn"]), rms_norm(c, p["g_out_conv"])], axis=-1)
    x = x + rms_norm(mix @ p["w_out"], p["g_post_mix"])
    h = rms_norm(x, p["g_pre_x"])
    qx = (h @ p["w_xq"]).reshape(B, T, N_XHEADS, XHEAD_DIM)
    s = jnp.einsum("bthd,bmhd->bhtm", qx, mem_k).astype(jnp.float32) * (XHEAD_DIM ** -0.5)
    pm = jax.nn.softmax(s, axis=-1)
    ox = jnp.einsum("bhtm,bmhd->bthd", pm.astype(mem_v.dtype), mem_v).reshape(B, T, D_MODEL)
    x = x + rms_norm(ox @ p["w_xo"], p["g_post_x"])
    h = rms_norm(x, p["g_pre_ffn"])
    up = h @ p["w_up"]
    act_in, lin = jnp.split(up, [D_FF], axis=-1)
    f_ctx = jnp.concatenate([ffn_ctx, act_in], axis=1)
    f = jax.nn.gelu(causal_dwconv(f_ctx, p["ffn_conv_w"])) * lin
    new_ffn = f_ctx[:, -(FFN_CONV - 1):]
    x = x + rms_norm(f @ p["w_down"], p["g_post_ffn"])
    return x, new_k, new_v, new_conv, new_ffn

def setup_inputs(seed: int = 0) -> dict:
    key = jax.random.key(seed)
    ks = jax.random.split(key, 40)
    f32 = jnp.float32

    def nrm(k, shape, scale):
        return jax.random.normal(k, shape, f32) * scale

    def gain(k, n):
        return 1.0 + 0.01 * jax.random.normal(k, (DEPTH, n), f32)

    wb = min(MAX_WINDOW, PAST_LEN)
    return {
        "x_prompt": nrm(ks[0], (BATCH, SEQ, D_MODEL), 1.0),
        "x_sample": nrm(ks[1], (DEC_BATCH, DEC_SEQ, D_MODEL), 1.0),
        "mem_prompt": nrm(ks[2], (BATCH, N_MEM, D_MODEL), 1.0),
        "cache_win_k": nrm(ks[3], (DEPTH, DEC_BATCH, wb, N_ATTN_HEADS, HEAD_DIM), 1.0),
        "cache_win_v": nrm(ks[4], (DEPTH, DEC_BATCH, wb, N_ATTN_HEADS, HEAD_DIM), 1.0),
        "state_conv": nrm(ks[5], (DEPTH, DEC_BATCH, CONV_KERNEL - 1, CONV_CH), 0.5),
        "state_ffn_conv": nrm(ks[6], (DEPTH, DEC_BATCH, FFN_CONV - 1, D_FF), 1.0),
        "cache_mem_k": nrm(ks[7], (DEPTH, DEC_BATCH, N_MEM, N_XHEADS, XHEAD_DIM), 1.0),
        "cache_mem_v": nrm(ks[8], (DEPTH, DEC_BATCH, N_MEM, N_XHEADS, XHEAD_DIM), 1.0),
        "g_pre_mix": gain(ks[9], D_MODEL),
        "w_in": nrm(ks[10], (DEPTH, D_MODEL, IN_COLS), D_MODEL ** -0.5),
        "conv_w": nrm(ks[11], (DEPTH, CONV_KERNEL, CONV_CH), CONV_KERNEL ** -0.5),
        "conv_b": nrm(ks[12], (DEPTH, CONV_CH), 0.01),
        "ln_conv_g": gain(ks[13], CONV_CH),
        "ln_conv_b": nrm(ks[14], (DEPTH, CONV_CH), 0.01),
        "g_out_attn": gain(ks[15], ATTN_WIDTH),
        "g_out_conv": gain(ks[16], CONV_CH),
        "w_out": nrm(ks[17], (DEPTH, D_MODEL, D_MODEL), D_MODEL ** -0.5),
        "g_post_mix": gain(ks[18], D_MODEL),
        "g_pre_x": gain(ks[19], D_MODEL),
        "g_mem": gain(ks[20], D_MODEL),
        "w_xq": nrm(ks[21], (DEPTH, D_MODEL, D_MODEL), D_MODEL ** -0.5),
        "w_mk": nrm(ks[22], (DEPTH, D_MODEL, D_MODEL), D_MODEL ** -0.5),
        "w_mv": nrm(ks[23], (DEPTH, D_MODEL, D_MODEL), D_MODEL ** -0.5),
        "w_xo": nrm(ks[24], (DEPTH, D_MODEL, D_MODEL), D_MODEL ** -0.5),
        "g_post_x": gain(ks[25], D_MODEL),
        "g_pre_ffn": gain(ks[26], D_MODEL),
        "w_up": nrm(ks[27], (DEPTH, D_MODEL, 2 * D_FF), D_MODEL ** -0.5),
        "ffn_conv_w": nrm(ks[28], (DEPTH, FFN_CONV, D_FF), FFN_CONV ** -0.5),
        "w_down": nrm(ks[29], (DEPTH, D_FF, D_MODEL), D_FF ** -0.5),
        "g_post_ffn": gain(ks[30], D_MODEL),
    }

def reference(x_prompt, x_sample, mem_prompt, cache_win_k, cache_win_v, state_conv, state_ffn_conv,
              cache_mem_k, cache_mem_v, g_pre_mix, w_in, conv_w, conv_b, ln_conv_g, ln_conv_b,
              g_out_attn, g_out_conv, w_out, g_post_mix, g_pre_x, g_mem, w_xq, w_mk, w_mv, w_xo,
              g_post_x, g_pre_ffn, w_up, ffn_conv_w, w_down, g_post_ffn):
    y_p, y_s = x_prompt, x_sample
    wk_p, wv_p, cv_p, ff_p, mk_p, mv_p = [], [], [], [], [], []
    wk_s, wv_s, cv_s, ff_s = [], [], [], []
    for l in range(DEPTH):
        p = {
            "g_pre_mix": g_pre_mix[l], "w_in": w_in[l], "conv_w": conv_w[l], "conv_b": conv_b[l],
            "ln_conv_g": ln_conv_g[l], "ln_conv_b": ln_conv_b[l], "g_out_attn": g_out_attn[l],
            "g_out_conv": g_out_conv[l], "w_out": w_out[l], "g_post_mix": g_post_mix[l],
            "g_pre_x": g_pre_x[l], "g_mem": g_mem[l], "w_xq": w_xq[l], "w_mk": w_mk[l],
            "w_mv": w_mv[l], "w_xo": w_xo[l], "g_post_x": g_post_x[l], "g_pre_ffn": g_pre_ffn[l],
            "w_up": w_up[l], "ffn_conv_w": ffn_conv_w[l], "w_down": w_down[l], "g_post_ffn": g_post_ffn[l],
        }
        mk, mv = memory_kv(mem_prompt, p)
        zc = jnp.zeros((y_p.shape[0], CONV_KERNEL - 1, CONV_CH), y_p.dtype)
        zf = jnp.zeros((y_p.shape[0], FFN_CONV - 1, D_FF), y_p.dtype)
        y_p, nk, nv, nc, nf = trunk_layer(y_p, True, None, None, zc, zf, mk, mv, p)
        wk_p.append(nk); wv_p.append(nv); cv_p.append(nc); ff_p.append(nf); mk_p.append(mk); mv_p.append(mv)
        y_s, nk, nv, nc, nf = trunk_layer(y_s, False, cache_win_k[l], cache_win_v[l], state_conv[l],
                                          state_ffn_conv[l], cache_mem_k[l], cache_mem_v[l], p)
        wk_s.append(nk); wv_s.append(nv); cv_s.append(nc); ff_s.append(nf)
    return (y_p, y_s,
            jnp.stack(wk_p), jnp.stack(wv_p), jnp.stack(cv_p), jnp.stack(ff_p), jnp.stack(mk_p), jnp.stack(mv_p),
            jnp.stack(wk_s), jnp.stack(wv_s), jnp.stack(cv_s), jnp.stack(ff_s))


_drawn_inputs = setup_inputs


def setup_inputs(seed=0):
    import zlib

    import numpy as np

    out = dict(_drawn_inputs(seed))
    spreads = {}
    factors = {'g_pre_mix': 4.926,
     'conv_b': 5.142,
     'ln_conv_g': 8.0,
     'ln_conv_b': 8.0,
     'g_out_attn': 8.0,
     'g_out_conv': 8.0,
     'g_post_mix': 7.304,
     'g_pre_x': 8.0,
     'g_mem': 5.876,
     'g_post_x': 8.0,
     'g_pre_ffn': 5.57,
     'g_post_ffn': 8.0}
    for name, (base, spread) in spreads.items():
        noise = np.random.default_rng([zlib.crc32(name.encode()), seed]).standard_normal(out[name].shape)
        drawn = base * np.exp(spread * noise) if base else spread * noise
        out[name] = __import__('jax').numpy.asarray(drawn.astype(out[name].dtype))
    for name, factor in factors.items():
        out[name] = (out[name] * factor).astype(out[name].dtype)
    return out
```

```python
from contextlib import ExitStack

import numpy as np
import concourse.bass as bass
from concourse import mybir
from concourse.alu_op_type import AluOpType as ALU

F32 = mybir.dt.float32
F32R = mybir.dt.float32r
ACT = mybir.ActivationFunctionType
AX = mybir.AxisListType

P = 128
D = 1024
NT = D // P
SEQ = 1024
BD, TD = 8, 4
NS = BD * TD
NTOK = SEQ + NS
CH = 3
CW = NTOK // CH
SP0 = SEQ - (CH - 1) * CW
TT = SEQ // P
H, DH = 8, 64
AW = H * DH
AT = AW // P
CC = D - AW
CT = CC // P
KW = 31
PAD = KW - 1
WB = 2048
DIL = ((128, 1), (512, 4), (2048, 16))
XH, XD = 4, 256
NM = 256
MT = NM // P
DF = 2816
FT = DF // P
EPS = 1e-6
SCALE = DH ** -0.5
XSCALE = XD ** -0.5
OLD = 384
NEAR = 512
KEYS = OLD + NEAR
KTILES = KEYS // P
MASKED = -1e30

PRM = (("g_pre_mix", 8), ("g_out_attn", 4), ("g_out_conv", 4), ("g_post_mix", 8), ("g_pre_x", 8), ("g_mem", 8),
       ("g_post_x", 8), ("g_pre_ffn", 8), ("g_post_ffn", 8), ("conv_b", 4), ("ln_conv_g", 4), ("ln_conv_b", 4))
PRM_AT, PRM_N = {}, 0
for _n, _k in PRM:
    PRM_AT[_n] = PRM_N
    PRM_N += _k


def log_count(distance):
    count = np.zeros(distance.shape, np.int64)
    for window, dil in DIL:
        count += (distance >= 0) & (distance <= window) & (distance % dil == 0)
    return np.where(count > 0, np.log(np.maximum(count, 1)) / SCALE, MASKED).astype(np.float32)


def prompt_bias():
    return log_count((TT - 1) * P + np.arange(P)[:, None] - np.arange(SEQ)[None, :])


def sample_bias():
    old = (16 * np.arange(OLD // 4)[:, None] + np.arange(4)[None, :]).ravel()
    near = WB - NEAR + np.arange(NEAR)
    idx = np.concatenate([old, near])
    t = np.tile(np.arange(TD), H)[:, None]
    cached = log_count(WB + t - idx[None, :])
    own = [np.where(np.arange(NS)[None, :] // TD == b, log_count(t - np.arange(NS)[None, :] % TD), MASKED) for b in range(BD)]
    return np.concatenate([cached] + own, axis=1).astype(np.float32)


SBW = KEYS + BD * NS


def pieces(c):
    out, g = [], c * CW
    while g < (c + 1) * CW:
        r = g % P
        n = min(P - r, (c + 1) * CW - g, (SEQ if g < SEQ else NTOK) - g)
        out.append((g // P, r, n, g - c * CW))
        g += n
    return out


SHARED = {"qbd_a": "qbd", "spt_a": "spt", "satt_a": "satt", "qbx_a": "qbx", "ams_a": "ams", "actx_p": "actx",
          "acar_p": "acar", "cvp": "cv", "cvs": "cv", "pt_a": "pt", "aev_p": "aev", "srd": "prd", "xrd": "prd", "mrd": "prd",
          "ar": "xr", "xm": "xmax", "mm": "mmax", "pm": "pmax", "sm": "smax", "mtk_t": "ztr", "att8_t": "cst_t",
          "fst_t": "cst_t", "prm_t": "cst_t", "mt": "h1t", "att_t": "h1t", "mhi": "h1hi", "mlo": "h1lo", "asd": "xsd",
          "ass": "xss", "csd": "std", "crs": "rstd", "mtok": "ztok", "mkv": "zt", "cmean": "csq_used", "att8": "att",
          "mexp": "sexp", "mpn": "spn", "mpt": "spt", "mptr": "sptr", "mpv": "spv", "msc": "ssc", "ktm": "kts", "xms": "ams"}


class Signals:

    def __init__(self, nc, ctx, counts):
        self.nc, self.ctx, self.counts = nc, ctx, counts
        self.sems, self.now, self.noted = {}, {}, {}

    def sem(self, name):
        name = SHARED.get(name, name)
        if name not in self.sems:
            self.sems[name] = self.ctx.enter_context(self.nc.semaphore(name))
        return self.sems[name]

    def mark(self, name, key, by=1):
        n = SHARED.get(name, name)
        self.now[n] = self.now.get(n, 0) + by
        assert (name, key) not in self.noted, (name, key)
        self.noted[name, key] = self.now[n]
        return self.sem(name), by

    def reached(self, name, key):
        return self.sem(name), self.counts[name, key] if self.counts else 1


def layout(nc, ctx, A, O, counts):
    S = Signals(nc, ctx, counts)
    mark, at = S.mark, S.reached
    base = -(-nc.sbuf_base // 32) * 32
    nc_at = nc.alloc_sbuf_tensor_at

    def place(name, off, shape, dt=F32):
        return nc_at(name, shape, dt, offset=base + off)

    small = [0]

    def sm(name, shape, dt=F32):
        n = 4
        for s in shape[1:]:
            n *= s
        t = place(name, small[0], shape, dt)
        small[0] += -(-n // 32) * 32
        return t

    ident = sm("ident", [P, P])
    ones_d = sm("ones_d", [P, P])
    ones_c = sm("ones_c", [P, P])
    prm = sm("prm", [P, PRM_N])
    cw = sm("cw", [P, KW, CT])
    fw = sm("fw", [P, 3, FT])
    sffn = sm("sffn", [P, BD * 2, FT])
    carry = sm("carry", [P, 2, FT])
    qbd = [sm(f"qbd{i}", [P, 160]) for i in range(2)]
    qbx = [sm(f"qbx{i}", [P, 144]) for i in range(2)]
    eps = sm("eps", [P, 1])
    ssx = sm("ssx", [P, 12, 2])
    rx = sm("rx", [P, 12])
    rx2 = sm("rx2", [P, 12])
    rx3 = sm("rx3", [P, 12])
    mx = sm("mx", [P, 2, 4])
    negm = sm("negm", [P, 4])
    den = sm("den", [P, 4])
    rden = sm("rden", [P, 4])
    TAB = 7168
    assert small[0] <= TAB
    RING = TAB + 8704
    MAIN = RING + 9 * 4096

    wt = place("wt", TAB, [P, SEQ])
    ws = place("ws", TAB + 4096, [H * TD, SBW])
    raw = [place(f"raw{i}", RING + 4096 * i, [P, 8, P]) for i in range(3)]
    whi = [place(f"whi{i}", RING + 4096 * (3 + i), [P, 8, P], F32R) for i in range(3)]
    wlo = [place(f"wlo{i}", RING + 4096 * (6 + i), [P, 8, P], F32R) for i in range(3)]

    def mn(name, off, shape, dt=F32):
        return place(name, MAIN + off, shape, dt)

    h1hi = mn("h1hi", 0, [P, NT, NTOK], F32R)
    h1lo = mn("h1lo", 33792, [P, NT, NTOK], F32R)
    QT = mn("QT", 67584, [P, AT, NTOK])
    VT = mn("VT", 67584, [P, AT, NTOK])
    KT = mn("KT", 84480, [P, AT, NTOK])
    V = mn("V", 101376, [P, TT + 1, AW])
    KS = mn("KS", 101376, [P, TT + 1, AW])
    U = mn("U", 119808, [P, CT, PAD + SEQ])
    US = mn("US", 136672, [P, CT, BD, PAD + TD])
    C = mn("C", 141024, [P, CT, NTOK])
    xt = [mn(f"xt{i}", 67584 + 4096 * i, [P, D]) for i in range(TT + 1)]
    junk = mn("junk", 157920, [P, 512])
    stage_u = mn("stage_u", 141024, [120, 2, CC])
    stage_p = mn("stage_p", 145120, [P, 3, P])
    stage_f = mn("stage_f", 146656, [P, 3, P])
    cached = [mn(f"cached{i}", o, [P, KTILES, AW]) for i, o in enumerate((0, 119808, 101376))]
    ATT = mn("ATT", 20480, [P, TT + 1, AW])
    Pp = [mn(f"Pp{i}", 38912 + 4096 * i, [P, SEQ]) for i in range(2)]
    PT = [mn(f"PT{i}", 47104 + 4096 * i, [P, SEQ]) for i in range(2)]
    Ps = mn("Ps", 38912, [H * TD, KEYS + NS])
    PTs = mn("PTs", 47104, [P, KTILES + 1, H * TD])
    attsT = mn("attsT", 51200, [P, AT, NS])
    usn = mn("usn", 51712, [P, CT, NS])
    KTS = mn("KTS", 55296 - 2048, [P, AT, KEYS])
    mtk = [mn(f"mtk{i}", 67584 + 4096 * i, [P, D]) for i in range(MT)]
    mhi = mn("mhi", 75776, [P, NT, NM], F32R)
    mlo = mn("mlo", 83968, [P, NT, NM], F32R)
    MVT = mn("MVT", 92160, [P, NT, NM])
    MKO = mn("MKO", 100352, [P, MT, D])
    MKT = mn("MKT", 112640, [P, NT, NM])
    MV = mn("MV", 120832, [P, MT, D])
    XT = [mn("XT0", 0, [P, NT, CW]), mn("XT1", 20480, [P, NT, CW]), mn("XT2", 31744, [P, NT, CW])]
    xtok = [mn(f"xtok{i}", o, [P, D]) for i, o in enumerate((11264, 15360, 43008))]
    OX = [place(f"OX{i}", TAB + 1408 * i, [P, CW]) for i in range(2)]
    Y = mn("Y", 50176, [P, NT, CW])
    RSX = mn("RSX", 61440, [P, CH, CW])
    RSTD = mn("RSTD", 65664, [P, CW])
    STD = mn("STD", 48640, [P, CW])
    RSC = mn("RSC", 50176, [P, CH, CW])
    SSUM = place("SSUM", TAB + 5824, [P, CW])
    SQ = [mn(f"SQ{i}", 129024 + 1408 * i, [P, CW]) for i in range(2)]
    SQf = [place(f"SQf{i}", TAB + 1504 * i, [P, CW]) for i in range(2)]
    op_hi = [mn(f"op_hi{i}", 67584 + 22528 * i, [P, NT, CW], F32R) for i in range(2)]
    op_lo = [mn(f"op_lo{i}", 78848 + 22528 * i, [P, NT, CW], F32R) for i in range(2)]
    PX = [mn(f"PX{i}", 131840 + 3072 * i, [P, 3, NM]) for i in range(2)]
    PTX = [mn(f"PTX{i}", 137984 + 2816 * i, [P, MT, CW]) for i in range(2)]
    KTm = mn("KTm", 143616, [P, NT, NM])
    vm = [mn("vm0", 151808, [P, MT, D]), mn("vm1", 120832, [P, MT, D])]
    kmraw = [[mn("kmraw00", 43008, [P, D]), mn("kmraw01", 11264, [P, D])],
             [mn("kmraw10", 112640, [P, D]), mn("kmraw11", 116736, [P, D])]]
    PTm = mn("PTm", 15360, [P, MT, 16])
    fhi = mn("fhi", 112640, [P, FT, CW], F32R)
    flo_a = mn("flo_a", 143616, [P, 11, CW], F32R)
    flo_b = mn("flo_b", 43008, [P, 4, CW], F32R)
    flo_c = mn("flo_c", 11264, [P, 6, CW], F32R)
    flo_d = place("flo_d", TAB + 7232, [P, 1, CW], F32R)
    flo = [flo_a[:, i] for i in range(11)] + [flo_b[:, i] for i in range(4)] + [flo_c[:, i] for i in range(6)] + [flo_d[:, 0]]
    aext = [place(f"aext{i}", TAB + 1504 * i, [P, 376]) for i in range(2)]
    cv = [place(f"cv{i}", TAB + 3008 + 1408 * i, [P, CW]) for i in range(2)]
    OT = [mn(f"OT{i}", 50176 + 2048 * i, [P, 512]) for i in range(4)]
    fst = mn("fst", 50176 + 8192, [P, 4, P])
    cst = mn("cst", 43008, [P, 2, CC])

    bank = [ctx.enter_context(nc.psum_tensor(f"bank{i}", [P, 512], F32)) for i in range(8)]

    def g_of(name, m):
        return prm[:, PRM_AT[name] + m:PRM_AT[name] + m + 1]

    units, unit_of = [], {}

    def add_unit(key, w, k0, nk, m):
        unit_of[key] = len(units)
        units.append((w[0, k0 * P:(k0 + nk) * P, m * P:(m + 1) * P].rearrange("(k p) n -> p k n", p=P), nk))

    order_in = []
    for i in range(CT):
        order_in += [("gate", i, 3 * AT + CT + i), ("a", i, 3 * AT + i)]
    order_in += [("k", i, AT + i) for i in range(AT)] + [("v", i, 2 * AT + i) for i in range(AT)]
    order_in += [("q", i, i) for i in range(AT)]
    for kind, i, col in order_in:
        add_unit((kind, i), A["w_in"], 0, NT, col)
    for kind in ("w_mk", "w_mv"):
        for m in range(NT):
            add_unit((kind, m), A[kind], 0, NT, m)
    for c in range(CH):
        for m in range(NT):
            add_unit(("out", c, m), A["w_out"], 0, NT, m)
    for c in range(CH):
        for kind, w in (("xq", "w_xq"), ("xo", "w_xo")):
            for m in range(NT):
                add_unit((kind, c, m), A[w], 0, NT, m)
    DOWN = ((0, 8), (8, 8), (16, 6))
    for c in range(CH):
        for j in range(FT):
            add_unit(("act", c, j), A["w_up"], 0, NT, j)
            add_unit(("lin", c, j), A["w_up"], 0, NT, FT + j)
        for m in range(NT):
            for k0, nk in DOWN:
                add_unit(("down", c, m, k0), A["w_down"], k0, nk, m)
    NU = len(units)
    FIRST_MEM = unit_of["w_mk", 0]

    STEPS = [(i, h) for i in range(TT) for h in range(H)]
    QTS = [[(0, P), (P, P), (2 * P, (CW if c < CH - 1 else SP0) - 2 * P)] for c in range(CH)]
    SLOT = {("mix", 0): 0, ("mix", 1): 1, ("mix", 2): 0, ("xq", 0): 1, ("xq", 1): 1, ("xq", 2): 1,
            ("xo", 0): 0, ("xo", 1): 0, ("xo", 2): 0, ("ffn", 0): 1, ("ffn", 1): 0, ("ffn", 2): 1}
    FREE = {("mix", 2): ("out", 0, 7), ("xq", 0): ("out", 1, 7), ("xq", 1): ("xq", 0, 7), ("xq", 2): ("xq", 1, 7),
            ("xo", 0): ("out", 2, 7), ("xo", 1): ("xo", 0, 7), ("xo", 2): ("xo", 1, 7),
            ("ffn", 0): ("xq", 2, 7), ("ffn", 1): ("xo", 2, 7), ("ffn", 2): ("lin", 0, FT - 1)}
    GAIN = {"xq": "g_pre_x", "ffn": "g_pre_ffn"}
    POST = {"out": "g_post_mix", "xo": "g_post_x", "down": "g_post_ffn"}
    XSLOT = [[0, 1, 2], [0, 1, 2, 0], [0, 1, 2, 0]]

    def bank_of(u):
        return u % 4

    def need_uc(eng, u, c):
        eng.wait_ge(*at(*(("unit", u) if c == CH - 1 else ("uc", (u, c)))))

    def y_free(eng, name, c):
        if name == "out":
            eng.wait_ge(*at(*(("cf", (CH - 1, CT - 1)) if c == 0 else ("x", ("out", c - 1, NT - 1)))))
        elif name == "xq":
            eng.wait_ge(*at("x", ("out", CH - 1, NT - 1) if c == 0 else ("xo", c - 1, NT - 1)))
        elif name == "xo":
            eng.wait_ge(*at("xsc", (c * XH + XH - 1, 2)))
            if c == CH - 1:
                eng.wait_ge(*at("qbx", BD - 1))
        elif c == 0:
            eng.wait_ge(*at("x", ("xo", CH - 1, NT - 1)))
        else:
            last = sum(2 * len(pieces(k)) for k in range(c))
            for g in range(last - 4, last):
                eng.wait_ge(*at(f"ot{g % 4}", g))

    block = ctx.enter_context(nc.Block())

    @block.sync
    def _(sp):
        def load(dst, src, name, key=0):
            sp.dma_start(dst, src).then_inc(*mark(name, key, 16))

        def weight(u):
            if u >= 3:
                sp.wait_ge(*at("w_lo", u - 3))
            w, nk = units[u]
            load(raw[u % 3][:, 0:nk, :], w, f"raw{u % 3}", u)

        def load_x(i):
            if i < TT:
                load(xt[i][:, :], A["x_prompt"][0, i * P:(i + 1) * P, :], f"x_in{i // 3}", i)
            else:
                load(xt[i][0:NS, :], A["x_sample"].rearrange("b t d -> (b t) d"), f"x_in{i // 3}", i)

        r = 0
        for n, k in PRM:
            load(stage_p[r:r + k, 0, :], A[n].rearrange("a (k p) -> (a k) p", p=P), "params", n)
            r += k
        for i in range(3):
            load_x(i)
        load(stage_p[0:KW * CT, 1, :], A["conv_w"].rearrange("a t (k p) -> (a t k) p", p=P), "params", "cw")
        load(stage_p[0:3 * FT, 2, :], A["ffn_conv_w"].rearrange("a t (k p) -> (a t k) p", p=P), "params", "fw")
        ffn_rows = A["state_ffn_conv"].rearrange("a b t (k p) -> (a b t k) p", p=P)
        for i in range(3):
            n = min(P, 16 * FT - i * P)
            load(stage_f[0:n, i, :], ffn_rows[i * P:i * P + n, :], "params", ("f", i))
        for i in range(2):
            load(stage_u[:, i, :], A["state_conv"].rearrange("a b t c -> (a b t) c")[i * 120:(i + 1) * 120, :], "params", ("u", i))
        load(ident[:, :], A["identity"], "params", "ident")
        weight(0)
        for i in range(3, TT + 1):
            load_x(i)
        for u in range(1, 3):
            weight(u)
        load(wt[:, :], A["prompt_bias"], "tables", "p")
        load(ws[:, :], A["sample_bias"], "tables", "s")
        for u in range(3, FIRST_MEM + 5):
            weight(u)
        def window(n):
            rows = A["cache_win_v" if n % 2 else "cache_win_k"][0, n // 2].rearrange("s h d -> s (h d)")
            dst, name = cached[n % 3], f"cached{n % 3}"
            load(dst[:, OLD // P:, :], rows[WB - NEAR:WB, :].rearrange("(a p) n -> p a n", p=P), name, (n, "near"))
            for a in range(OLD // P):
                load(dst[:, a, :], rows.rearrange("(g r) n -> g r n", r=16)[a * 32:(a + 1) * 32, 0:4, :], name, (n, a))

        sp.wait_ge(*at("unit", FIRST_MEM - 1))
        window(0)
        sp.wait_ge(*at("conv", "end"))
        sp.wait_ge(*at("cst_t", 0))
        window(1)
        sp.wait_ge(*at("pv", len(STEPS) - 1))
        sp.wait_ge(*at("v_out", TT))
        window(2)
        for n in range(3, 2 * BD):
            b = (n - 3) // 2
            if (n - 3) % 2:
                sp.wait_ge(*at("spv", b))
            else:
                sp.wait_ge(*at("ktr", b * KTILES + KTILES - 1))
            window(n)
        sp.wait_ge(*at("spv", BD - 1))
        sp.wait_ge(*at("pv", len(STEPS) - 1))
        for i in range(MT):
            load(mtk[i][:, :], A["mem_prompt"][0, i * P:(i + 1) * P, :], f"mem_in{i}")
        keys = list(unit_of)
        for u in range(FIRST_MEM + 5, NU):
            key = keys[u]
            if key[0] == "out" and key[2] == 5:
                c = key[1]
                if c > 0:
                    sp.wait_ge(*at("xtr", (c - 1, len(pieces(c - 1)) - 1, 1)))
                else:
                    sp.wait_ge(*at("cst_out", BD - 1))
                for s, (i, r, n, off) in zip(XSLOT[c], pieces(c)):
                    if i < TT:
                        load(xtok[s][r:r + n, :], A["x_prompt"][0, i * P + r:i * P + r + n, :], f"xtok{s}", (c, i))
                    else:
                        load(xtok[s][0:NS, :], A["x_sample"].rearrange("b t d -> (b t) d"), f"xtok{s}", (c, i))
            if key == ("xo", CH - 1, 3):
                sp.wait_ge(*at("op_lo", ("mix", 2, NT - 1)))
                sp.wait_ge(*at("xtr", (CH - 1, len(pieces(CH - 1)) - 1, 1)))
                for b in range(BD):
                    for mt in range(MT):
                        if b >= 2:
                            sp.wait_ge(*at("mtr", (b - 2, mt, 1)))
                        elif b == 1:
                            sp.wait_ge(*at("xsc", (CH * XH - 1, 2)))
                        load(kmraw[b % 2][mt][:, :], A["cache_mem_k"][0, b, mt * P:(mt + 1) * P].rearrange("m h d -> m (h d)"), f"kmraw{b % 2}{mt}", b)
                    if b >= 2:
                        sp.wait_ge(*at("mpv", b - 2))
                    elif b == 1:
                        sp.wait_ge(*at("xpv", (CH * XH - 1, 1)))
                        sp.wait_ge(*at("mv_out", MT - 1))
                    load(vm[b % 2][:, :, :], A["cache_mem_v"][0, b].rearrange("(t p) h d -> p t (h d)", p=P), f"vm{b % 2}", b)
            weight(u)

    @block.gpsimd
    def _(pool):
        pool.memset(ones_d[:, :], 1.0 / D).then_inc(*mark("const", "od"))
        pool.memset(ones_c[:, :], 1.0 / CC).then_inc(*mark("const", "oc"))
        pool.memset(eps[:, :], EPS).then_inc(*mark("const", "eps"))
        pool.memset(carry[:, :, :], 0.0).then_inc(*mark("const", "carry"))
        for i in range(2):
            pool.memset(qbd[i][:, :], 0.0).then_inc(*mark("const", ("qbd", i)))
            pool.memset(qbx[i][:, :], 0.0).then_inc(*mark("const", ("qbx", i)))
        pool.memset(ssx[:, :, :], 1.0).then_inc(*mark("const", "ssx"))
        pool.memset(U[:, :, 0:PAD], 0.0).then_inc(*mark("const", "all"))
        for u in range(NU):
            nk = units[u][1]
            pool.wait_ge(*at("w_hi", u))
            pool.tensor_tensor(wlo[u % 3][:, 0:nk, :], raw[u % 3][:, 0:nk, :], whi[u % 3][:, 0:nk, :].bitcast(F32), ALU.subtract).then_inc(*mark("w_lo", u))

    @block.scalar
    def _(act):
        nxt = [0]

        def split_to(u):
            while nxt[0] <= min(u, NU - 1):
                v = nxt[0]
                act.wait_ge(*at(f"raw{v % 3}", v))
                if v >= 3:
                    act.wait_ge(*at("unit", v - 3))
                nk = units[v][1]
                act.activation(whi[v % 3][:, 0:nk, :], raw[v % 3][:, 0:nk, :], ACT.Copy).then_inc(*mark("w_hi", v))
                nxt[0] += 1

        act.wait_ge(*at("const", "all"))
        act.wait_ge(*at("params", "ident"))
        for gidx in range(3):
            for i in range(3 * gidx, 3 * gidx + 3):
                n = P if i < TT else NS
                act.wait_ge(*at(f"x_in{i // 3}", 3 * (i // 3) + 2))
                for hf in range(2):
                    if i or hf:
                        act.wait_ge(*at("xss", (i, 0) if hf else (i - 1, 1)))
                    act.activation(junk[0:n, :], xt[i][0:n, hf * 512:(hf + 1) * 512], ACT.Square,
                                        accum_out=ssx[0:n, i, hf:hf + 1]).then_inc(*mark("xss", (i, hf)))
            act.wait_ge(*at("xms", gidx))
            act.activation(rx2[:, 3 * gidx:3 * gidx + 3], rx[:, 3 * gidx:3 * gidx + 3], ACT.Sqrt, bias=eps[:, :], scale=1.0 / D).then_inc(*mark("xsd", gidx))
        split_to(1)
        n = 0
        for c in range(CH):
            for m in range(NT):
                act.wait_ge(*at("h1t", (c, m)))
                act.activation(h1hi[:, m, c * CW:(c + 1) * CW], bank[4 + n % 2][:, 0:CW], ACT.Copy, scale=g_of("g_pre_mix", m)).then_inc(*mark("h1hi", (c, m)))
                n += 1
        for kind, i, _ in order_in:
            u = unit_of[kind, i]
            split_to(u + 2)
            for c in range(CH):
                b = bank[3 * (u % 2) + c]
                cols = slice(c * CW, (c + 1) * CW)
                if kind == "gate":
                    need_uc(act, u, c)
                    n = SP0 if c == CH - 1 else CW
                    act.activation(U[:, i, PAD + c * CW:PAD + c * CW + n], b[:, 0:n], ACT.Sigmoid).then_inc(*mark("sig", (i, c)))
                    if c == CH - 1:
                        act.activation(US[:, i, :, PAD:], b[:, SP0:CW].rearrange("p (b t) -> p b t", t=TD), ACT.Sigmoid).then_inc(*mark("sig", (i, "s")))
                elif kind in ("k", "v", "q"):
                    need_uc(act, u, c)
                    if kind == "q" and i == 0 and c == 0:
                        act.wait_ge(*at("ztok", ("v", AT - 1, 2)))
                    act.activation({"k": KT, "v": VT, "q": QT}[kind][:, i, cols], b[:, 0:CW], ACT.Copy).then_inc(*mark("zt", (kind, i, c)))
            if kind == "v" and i == 0:
                act.wait_ge(*at("ztok", ("k", AT - 1, 2)))
                for t in range(TT):
                    act.dma_start(O["win_k_p"][0, 0, t * P:(t + 1) * P].rearrange("s h d -> s (h d)"), KS[:, t, :]).then_inc(*mark("ks_out", t, 16))
                act.dma_start(O["win_k_s"][0].rearrange("b t h d -> (b t) (h d)"), KS[0:NS, TT, :]).then_inc(*mark("ks_out", TT, 16))
            if kind == "q" and i == 0:
                for t in range(TT):
                    act.dma_start(O["win_v_p"][0, 0, t * P:(t + 1) * P].rearrange("s h d -> s (h d)"), V[:, t, :]).then_inc(*mark("v_out", t, 16))
                act.dma_start(O["win_v_s"][0].rearrange("b t h d -> (b t) (h d)"), V[0:NS, TT, :]).then_inc(*mark("v_out", TT, 16))

        steps = STEPS
        for s in range(len(steps) + 1):
            if s < len(steps):
                i, h = steps[s]
                act.wait_ge(*at("pmax", s))
                n = (i + 1) * P
                act.activation(Pp[s % 2][:, 0:n], Pp[s % 2][:, 0:n], ACT.Exp, bias=negm[:, s % 2:s % 2 + 1], accum_out=den[:, s % 2:s % 2 + 1]).then_inc(*mark("pexp", s))
            if s >= 1:
                i, h = steps[s - 1]
                q = (s - 1) % 2
                act.wait_ge(*at("ptr", s - 1))
                if s >= 3:
                    act.wait_ge(*at("pv", s - 3))
                n = (i + 1) * P
                last = act.activation(PT[q][:, 0:min(n, 512)], bank[4][:, 0:min(n, 512)], ACT.Copy)
                if n > 512:
                    last.then_inc(*mark("pt_a", s - 1))
                    last = act.activation(PT[q][:, 512:n], bank[5][:, 0:n - 512], ACT.Copy)
                last.then_inc(*mark("pt", s - 1))
        for b in range(BD + 1):
            if b < BD:
                for a in range(KTILES):
                    n = b * KTILES + a
                    act.wait_ge(*at("ktr", n))
                    if a == 0 and b > 0:
                        act.wait_ge(*at("ssc", b - 1))
                    if n == 0:
                        act.wait_ge(*at("pv", len(steps) - 1))
                    act.activation(KTS[:, :, a * P:(a + 1) * P], bank[n % 4][:, :].rearrange("p (k n) -> p k n", k=AT), ACT.Copy).then_inc(*mark("kts", n))
                act.wait_ge(*at("smax", b))
                act.activation(Ps[:, :], Ps[:, :], ACT.Exp, bias=negm[0:H * TD, 2:3], accum_out=den[0:H * TD, 2:3]).then_inc(*mark("sexp", b))
        split_to(FIRST_MEM + 2)
        for i in range(MT):
            act.wait_ge(*at(f"mem_in{i}", 0))
            for hf in range(2):
                act.wait_ge(*at("xss", (9 + i, 0) if hf else (8 + i, 1)))
                act.activation(junk[:, :], mtk[i][:, hf * 512:(hf + 1) * 512], ACT.Square, accum_out=ssx[:, 9 + i, hf:hf + 1]).then_inc(*mark("xss", (9 + i, hf)))
        act.wait_ge(*at("att8", 0))
        for i in range(TT + 1):
            n = P if i < TT else NS
            act.wait_ge(*at(*(("ass", i - 1) if i else ("xss", (8 + MT, 1)))))
            act.activation(junk[0:n, :], ATT[0:n, i, :], ACT.Square, accum_out=ssx[0:n, i, 0:1]).then_inc(*mark("ass", i))
        act.wait_ge(*at("ams", 0))
        act.activation(rx2[:, 0:11], rx[:, 0:11], ACT.Sqrt, bias=eps[:, :]).then_inc(*mark("asd", 0))
        for m in range(NT):
            act.wait_ge(*at("mt", m))
            act.activation(mhi[:, m, :], bank[m % 2][:, 0:NM], ACT.Copy, scale=g_of("g_mem", m)).then_inc(*mark("mhi", m))

        def ln_steps():
            n = 0
            for c in range(CH):
                for k in range(CT):
                    act.wait_ge(*at("cc", (c, k)))
                    if n >= 2:
                        act.wait_ge(*at("csq_used", n - 2))
                    else:
                        act.wait_ge(*at("spv", BD - 1))
                    act.activation(SQ[n % 2][:, :], C[:, k, c * CW:(c + 1) * CW], ACT.Square).then_inc(*mark("csq", n))
                    n += 1
                    yield
                act.wait_ge(*at("csq_used", n - 1))
                if c > 0:
                    act.wait_ge(*at("crs", (0, c - 1)))
                act.activation(STD[:, :], bank[6][:, 0:CW], ACT.Sqrt, bias=eps[:, :]).then_inc(*mark("csd", (0, c)))
                yield
            for c in range(CH):
                for k in range(CT):
                    act.wait_ge(*at("cn", (c, k)))
                    cols = C[:, k, c * CW:(c + 1) * CW]
                    act.activation(cols, cols, ACT.Silu, bias=g_of("ln_conv_b", k), scale=g_of("ln_conv_g", k)).then_inc(*mark("cs", (c, k)))
                    yield
            for c in range(CH):
                for k in range(CT):
                    act.wait_ge(*at("csq_used", n - 2))
                    if c == 0:
                        act.wait_ge(*at("cs", (CH - 1, CT - 1)))
                    act.activation(SQ[n % 2][:, :], C[:, k, c * CW:(c + 1) * CW], ACT.Square).then_inc(*mark("csq", n))
                    n += 1
                    yield
                act.wait_ge(*at("csq_used", n - 1))
                act.wait_ge(*at("crs", (0, CH - 1) if c == 0 else (1, c - 1)))
                act.activation(STD[:, :], bank[6][:, 0:CW], ACT.Sqrt, bias=eps[:, :]).then_inc(*mark("csd", (1, c)))
                yield

        for kind in ("w_mk", "w_mv"):
            for m in range(NT):
                u = unit_of[kind, m]
                split_to(u + 2)
                act.wait_ge(*at("unit", u))
                if m == 0 and kind == "w_mk":
                    act.wait_ge(*at("v_out", TT))
                    act.wait_ge(*at("conv", "end"))
                    act.wait_ge(*at("cst", 1))
                act.activation((MKT if kind == "w_mk" else MVT)[:, m, :], bank[2 + u % 2][:, 0:NM], ACT.Copy).then_inc(*mark("mkv", (kind, m)))
        for _ in ln_steps():
            pass
        act.wait_ge(*at("mtok", ("w_mv", NT - 1)))
        for mt in range(MT):
            act.dma_start(O["mem_k"][0, 0, mt * P:(mt + 1) * P].rearrange("m h d -> m (h d)"), MKO[:, mt, :]).then_inc(*mark("mko_out", mt, 16))
            act.dma_start(O["mem_v"][0, 0, mt * P:(mt + 1) * P].rearrange("m h d -> m (h d)"), MV[:, mt, :]).then_inc(*mark("mv_out", mt, 16))
        act.wait_ge(*at("cst", 1))
        act.dma_start(O["conv_p"][0, 0], cst[0:PAD, 0, :]).then_inc(*mark("cst_out", "p", 16))
        for b in range(BD):
            act.dma_start(O["conv_s"][0, b, PAD - TD:PAD, :], cst[b * TD:(b + 1) * TD, 1, :]).then_inc(*mark("cst_out", b, 16))
        act.dma_start(O["conv_s"][0, :, 0:PAD - TD, :], A["state_conv"][0, :, TD:PAD, :]).then_inc(*mark("out", "cs", 16))
        act.wait_ge(*at("mko_out", MT - 1))

        def mix(c):
            s = c % 2
            if c == 2:
                act.wait_ge(*at("unit", unit_of["out", 0, NT - 1]))
            for m in range(AT):
                act.wait_ge(*at("att_t", (c, m)))
                act.activation(op_hi[s][:, m, :], bank[4 + (c * AT + m) % 2][:, 0:CW], ACT.Copy, scale=g_of("g_out_attn", m)).then_inc(*mark("op_hi", ("mix", c, m)))
            for m in range(CT):
                act.wait_ge(*at("cf", (c, m)))
                act.activation(op_hi[s][:, AT + m, :], C[:, m, c * CW:(c + 1) * CW], ACT.Copy, scale=g_of("g_out_conv", m)).then_inc(*mark("op_hi", ("mix", c, AT + m)))

        sqn = [0]
        last_rstd = [None]

        def square(src, sq):
            n = sqn[0]
            act.wait_ge(*at("sqsum", n - 2)) if n >= 2 else act.wait_ge(*at("csq_used", 2 * CH * CT - 1))
            act.activation(sq[n % 2][:, :], src, ACT.Square).then_inc(*mark("sq", n))
            sqn[0] += 1

        def root(key):
            act.wait_ge(*at("means", key))
            if last_rstd[0]:
                act.wait_ge(*at("rstd", last_rstd[0]))
            else:
                act.wait_ge(*at("crs", (1, CH - 1)))
            act.activation(STD[:, :], bank[6][:, 0:CW], ACT.Sqrt, bias=eps[:, :]).then_inc(*mark("std", key))
            last_rstd[0] = key

        def evac_y(name, c, m, u, b, sq):
            act.wait_ge(*at("unit", u))
            if m == 0:
                y_free(act, name, c)
            act.activation(Y[:, m, :], bank[b][:, 0:CW], ACT.Copy).then_inc(*mark("y", (name, c, m)))
            if sq is not None:
                act.wait_ge(*at("y", (name, c, m)))
                square(Y[:, m, :], sq)

        def update(name, c, u):
            split_to(u + 3)
            if name == "out":
                for k, (i, r, n, off) in enumerate(pieces(c)):
                    for hf in range(2):
                        act.wait_ge(*at("xtr", (c, k, hf)))
                        act.activation(XT[c][:, 4 * hf:4 * hf + 4, off:off + n], bank[4 + hf][:, :].rearrange("p (k n) -> p k n", k=4)[:, :, 0:n], ACT.Copy).then_inc(*mark("xcp", (c, k, hf)))
            root((name, c, "y"))
            for m in range(NT):
                act.wait_ge(*at("x", (name, c, m)))
                square(XT[c][:, m, :], SQ)
                if m == 3:
                    split_to(u + 4)
                if m == 5:
                    split_to(u + 5)
            root((name, c, "x"))

        def operand(name, c):
            s = SLOT[name, c]
            act.wait_ge(*at("unit", unit_of[FREE[name, c]]))
            for m in range(NT):
                act.wait_ge(*at("opx", (name, c, m)))
                act.activation(op_hi[s][:, m, :], OX[m % 2][:, :], ACT.Copy, scale=g_of(GAIN[name], m)).then_inc(*mark("op_hi", (name, c, m)))

        mix(0)
        mix(1)
        for c in range(CH):
            for m in range(NT):
                u = unit_of["out", c, m]
                split_to(u + 2)
                evac_y("out", c, m, u, bank_of(u), SQ)
            update("out", c, u)
            if c == 0:
                mix(2)
            if c == 1:
                operand("xq", 0)
        for c in range(CH):
            for m in range(NT):
                u = unit_of["xq", c, m]
                split_to(u + 2)
                evac_y("xq", c, m, u, bank_of(u), None)
            qts = QTS[c]
            for h in range(XH):
                g = c * XH + h
                for t, (q0, qn) in enumerate(qts):
                    act.wait_ge(*at("xmax", (g, max(t, 1))))
                    bk, o = (0, t * NM) if t < 2 else (1, 0)
                    act.activation(PX[g % 2][0:qn, t, :], bank[2 * (g % 2) + bk][0:qn, o:o + NM], ACT.Exp, bias=negm[0:qn, t:t + 1], scale=XSCALE,
                                        accum_out=den[0:qn, t:t + 1]).then_inc(*mark("xexp", (g, t)))
                for mt in range(MT):
                    act.wait_ge(*at("xptr", (g, mt)))
                    if g >= 2:
                        act.wait_ge(*at("xpv", (g - 2, 1)))
                    n = CW if c < 2 else SP0
                    act.activation(PTX[g % 2][:, mt, 0:n], bank[4 + mt][:, 0:n], ACT.Copy).then_inc(*mark("xpt", (g, mt)))
                for e in range(2):
                    act.wait_ge(*at("xpv", (g, e)))
                    n = CW if c < 2 else SP0
                    act.activation(op_hi[0][:, 2 * h + e, 0:n], bank[6 + e][:, 0:n], ACT.Copy).then_inc(*mark("op_hi", ("xo", c, 2 * h + e)))
            if c == CH - 1:
                for b in range(BD):
                    for mt in range(MT):
                        for hf in range(2):
                            act.wait_ge(*at("mtr", (b, mt, hf)))
                            if mt == 0 and hf == 0 and b > 0:
                                act.wait_ge(*at("msc", b - 1))
                            act.activation(KTm[:, 4 * hf:4 * hf + 4, mt * P:(mt + 1) * P], bank[2 * mt + hf][:, :].rearrange("p (k n) -> p k n", k=4), ACT.Copy).then_inc(*mark("ktm", (b, mt, hf)))
                    act.wait_ge(*at("mmax", b))
                    act.activation(PX[0][0:16, 0, :], bank[4][0:16, 0:NM], ACT.Exp, bias=negm[0:16, 3:4], scale=XSCALE, accum_out=den[0:16, 3:4]).then_inc(*mark("mexp", b))
                act.wait_ge(*at("mpv", BD - 1))
                act.activation(op_hi[0][:, :, SP0:CW], bank[7][:, 0:NT * NS].rearrange("p (k n) -> p k n", k=NT), ACT.Copy).then_inc(*mark("op_hi", ("xo", c, "s")))
            if c < CH - 1:
                operand("xq", c + 1)
            else:
                operand("ffn", 0)
            for m in range(NT):
                u = unit_of["xo", c, m]
                split_to(u + 2)
                evac_y("xo", c, m, u, bank_of(u), SQ)
            update("xo", c, u)
        operand("ffn", 1)
        otn = 0
        for c in range(CH):
            def gelu(j):
                act.wait_ge(*at("cv", (c, j, 2)))
                act.activation(cv[j % 2][:, :], cv[j % 2][:, :], ACT.Gelu_apprx_tanh).then_inc(*mark("gelu", (c, j)))

            def f_high(j):
                act.wait_ge(*at("mv_out", MT - 1))
                act.wait_ge(*at("fmul", (c, j)))
                act.activation(fhi[:, j, :], cv[j % 2][:, :], ACT.Copy).then_inc(*mark("fhi", (c, j)))

            for j in range(FT):
                u = unit_of["act", c, j]
                split_to(u + 2)
                act.wait_ge(*at("unit", u))
                a = aext[j % 2]
                if j >= 2:
                    act.wait_ge(*at("acar", (c, j - 2)))
                elif c > 0:
                    act.wait_ge(*at("sqsum", sqn[0] - 1))
                    if c == 1:
                        act.wait_ge(*at("op_lo", ("ffn", 2, NT - 1)))
                else:
                    act.wait_ge(*at("op_lo", ("ffn", 1, NT - 1)))
                n = CW if c < 2 else SP0
                ins = act.activation(a[:, 2:2 + n], bank[u % 4][:, 0:n], ACT.Copy)
                if c == 2:
                    ins.then_inc(*mark("aev_p", (c, j)))
                    ins = act.activation(a[:, 2 + SP0:2 + SP0 + 48].rearrange("p (b t) -> p b t", t=6)[:, :, 2:6],
                                         bank[u % 4][:, SP0:CW].rearrange("p (b t) -> p b t", t=TD), ACT.Copy)
                ins.then_inc(*mark("aev", (c, j)))
                split_to(u + 3)
                gelu(j)
                f_high(j)
            for m in range(NT):
                for k0, nk in DOWN:
                    u = unit_of["down", c, m, k0]
                    split_to(u + 2)
                if m == 0:
                    act.wait_ge(*at("acar", (c, FT - 1)))
                evac_y("down", c, m, u, m % 4, SQf)
            split_to(u + 3)
            root(("down", c, "y"))
            split_to(u + 5)
            for k, (i, r, n, off) in enumerate(pieces(c)):
                for hf in range(2):
                    g = otn
                    otn += 1
                    act.wait_ge(*at("otr", g))
                    if g >= 4:
                        act.wait_ge(*at(f"ot{g % 4}", g - 4))
                    act.activation(OT[g % 4][0:n, :], bank[4 + g % 2][0:n, :], ACT.Copy).then_inc(*mark("ot_ev", g))
                    act.wait_ge(*at("ot_ev", g))
                    dst = (O["y_p"][0, i * P + r:i * P + r + n, hf * 512:(hf + 1) * 512] if i < TT else
                           O["y_s"].rearrange("b t d -> (b t) d")[:, hf * 512:(hf + 1) * 512])
                    act.dma_start(dst, OT[g % 4][0:n, :]).then_inc(*mark(f"ot{g % 4}", g, 16))
            if c == 0:
                operand("ffn", 2)
        for t in range(4):
            act.wait_ge(*at("fst", t))
        act.dma_start(O["ffn_p"].rearrange("a b t (k p) -> (a b t k) p", p=P), fst[0:2 * FT, 3, :]).then_inc(*mark("out", "fp", 16))
        rows = O["ffn_s"].rearrange("a b t (k p) -> (a b t k) p", p=P)
        for t in range(3):
            n = min(P, 16 * FT - t * P)
            act.dma_start(rows[t * P:t * P + n, :], fst[0:n, t, :]).then_inc(*mark("out", ("fs", t), 16))
        act.wait_ge(*at("out", ("fs", 2)))
        act.wait_ge(*at("ks_out", TT))
        act.wait_ge(*at("v_out", TT))
        act.wait_ge(*at("mko_out", MT - 1))
        act.wait_ge(*at("mv_out", MT - 1))
        act.wait_ge(*at("cst_out", BD - 1))
        for g in range(otn - 4, otn):
            act.wait_ge(*at(f"ot{g % 4}", g))

    @block.tensor
    def _(pe):
        reader = {}

        def take(b, name, key):
            if b in reader:
                pe.wait_ge(*at(*reader[b]))
            reader[b] = (name, key)

        def turn(out, in_, r=0):
            n = in_.shape[0]
            return pe.transpose(out, in_, ident[r:r + n, r:r + n])

        def mm(out, lhsT, rhs, first, last):
            return pe.matmul(out, lhsT, rhs, start=first, stop=last)

        def split_product(out, u, hi, lo, k0=0, first=True, last=True):
            nk, s = units[u][1], u % 3
            for k in range(nk):
                mm(out, whi[s][:, k, :], hi(k), first and k == 0, False)
                mm(out, whi[s][:, k, :], lo(k), False, False)
                ins = mm(out, wlo[s][:, k, :], hi(k), False, last and k == nk - 1)
            return ins

        pe.wait_ge(*at("params", "ident"))
        turn(bank[7][:, 0:PRM_N], stage_p[0:PRM_N, 0, :])
        turn(bank[7][:, PRM_N:PRM_N + KW * CT], stage_p[0:KW * CT, 1, :])
        turn(bank[7][:, 200:200 + 3 * FT], stage_p[0:3 * FT, 2, :]).then_inc(*mark("prm_t", 0))
        for i in range(3):
            n = min(P, 16 * FT - i * P)
            ins = turn(bank[4][:, i * P:i * P + n], stage_f[0:n, i, :])
        ins.then_inc(*mark("prm_t", 1))
        for i in range(2):
            for k in range(CT):
                ins = turn(bank[5 + i][:, k * 120:(k + 1) * 120], stage_u[:, i, k * P:(k + 1) * P])
            ins.then_inc(*mark("prm_t", 2 + i))
        for b in (4, 5, 6, 7):
            reader[b] = ("prm", "end")
        n = 0
        for c in range(CH):
            for m in range(NT):
                take(4 + n % 2, "h1lo", (c, m))
                for (i, r, rows, off) in pieces(c):
                    pe.wait_ge(*at("xn", i))
                    ins = turn(bank[4 + n % 2][:, off:off + rows], xt[i][r:r + rows, m * P:(m + 1) * P], r)
                ins.then_inc(*mark("h1t", (c, m)))
                n += 1
        def turn_kv(kind, i):
            src = KT if kind == "k" else VT
            for grp in range(3):
                take(6 + grp % 2, "ztok", (kind, i, grp))
                if grp == 0:
                    pe.wait_ge(*at("zt", (kind, i, CH - 1)))
                if grp < 2:
                    for t in range(4):
                        g = (4 * grp + t) * P
                        ins = turn(bank[6 + grp][:, t * P:(t + 1) * P], src[:, i, g:g + P])
                else:
                    ins = turn(bank[6][0:NS, 0:P], src[:, i, SEQ:NTOK])
                ins.then_inc(*mark("ztr", (kind, i, grp)))

        before = None
        for kind, i, _ in order_in:
            u = unit_of[kind, i]
            for c in range(CH):
                cols = slice(c * CW, (c + 1) * CW)
                if kind == "gate":
                    rd = ("sig", (i, "s" if c == CH - 1 else c))
                elif kind == "a":
                    rd = ("u", (i, "s" if c == CH - 1 else c))
                else:
                    rd = ("zt", (kind, i, c))
                take(3 * (u % 2) + c, *rd)
                if c == 0:
                    pe.wait_ge(*at("w_lo", u))
                if u == 0:
                    pe.wait_ge(*at("h1lo", (c, NT - 1)))
                ins = split_product(bank[3 * (u % 2) + c][:, 0:CW], u, lambda k: h1hi[:, k, cols], lambda k: h1lo[:, k, cols])
                ins.then_inc(*mark("unit", u)) if c == CH - 1 else ins.then_inc(*mark("uc", (u, c)))
            if before and before[0] in ("k", "v"):
                turn_kv(*before)
            before = (kind, i)
        pe.wait_ge(*at("zt", ("q", AT - 1, CH - 1)))

        for s in range(len(STEPS) + 2):
            if s < len(STEPS):
                i, h = STEPS[s]
                hp, rows = h // 2, slice(64 * (h % 2), 64 * (h % 2) + 64)
                n = (i + 1) * P
                for part in range(-(-n // 512)):
                    k0, k1 = part * 512, min(n, part * 512 + 512)
                    take(2 * (s % 2) + part, "pm", (s, part))
                    ins = mm(bank[2 * (s % 2) + part][:, 0:k1 - k0], QT[rows, hp, i * P:(i + 1) * P], KT[rows, hp, k0:k1], True, True)
                ins.then_inc(*mark("score", s))
            if 1 <= s <= len(STEPS):
                i, h = STEPS[s - 1]
                pe.wait_ge(*at("pexp", s - 1))
                q = (s - 1) % 2
                take(4, "pt_a" if i >= 4 else "pt", s - 1)
                if i >= 4:
                    take(5, "pt", s - 1)
                for blk in range(i + 1):
                    ins = turn(bank[4 + blk // 4][:, (blk % 4) * P:(blk % 4 + 1) * P], Pp[q][:, blk * P:(blk + 1) * P])
                ins.then_inc(*mark("ptr", s - 1))
            if s >= 2:
                i, h = STEPS[s - 2]
                q = s % 2
                pe.wait_ge(*at("pt", s - 2))
                take(6 + q, "att", s - 2)
                for blk in range(i + 1):
                    ins = mm(bank[6 + q][:, 0:DH], PT[q][:, blk * P:(blk + 1) * P], V[:, blk, h * DH:(h + 1) * DH], blk == 0, blk == i)
                ins.then_inc(*mark("pv", s - 2))
        take(6, "cst", 0)
        pe.wait_ge(*at("u", (CT - 1, "s")))
        for k in range(CT):
            ins = turn(bank[6][0:PAD, k * P:(k + 1) * P], U[:, k, SEQ:SEQ + PAD])
        ins.then_inc(*mark("cst_t", 0))
        take(7, "cst", 1)
        pe.wait_ge(*at("usn", 0))
        for k in range(CT):
            ins = turn(bank[7][0:NS, k * P:(k + 1) * P], usn[:, k, :])
        ins.then_inc(*mark("cst_t", 1))

        def turn_keys(b):
            for a in range(KTILES):
                n = b * KTILES + a
                take(n % 4, "kts", n)
                if a == 0:
                    pe.wait_ge(*at(f"cached{2 * b % 3}", (2 * b, OLD // P - 1)))
                for k in range(AT):
                    ins = turn(bank[n % 4][:, k * P:(k + 1) * P], cached[2 * b % 3][:, a, k * P:(k + 1) * P])
                ins.then_inc(*mark("ktr", n))

        def scores(b):
            pe.wait_ge(*at("kts", b * KTILES + KTILES - 1))
            pe.wait_ge(*at("qbd", b))
            take(4, "sm", (b, 0))
            take(5, "sm", (b, 2))
            R = H * TD
            for out, rhs in ((bank[4][0:R, 0:512], lambda k: KTS[:, k, 0:512]), (bank[5][0:R, 0:KEYS - 512], lambda k: KTS[:, k, 512:KEYS]),
                             (bank[5][0:R, KEYS - 512:KEYS - 512 + NS], lambda k: KT[:, k, SEQ:NTOK])):
                for k in range(AT):
                    ins = mm(out, qbd[b % 2][:, k * R:(k + 1) * R], rhs(k), k == 0, k == AT - 1)
            ins.then_inc(*mark("ssc", b))

        def values(b):
            R = H * TD
            pe.wait_ge(*at("spn", b))
            take(6, "spt", b)
            for a in range(KTILES):
                turn(bank[6][:, a * R:(a + 1) * R], Ps[:, a * P:(a + 1) * P])
            turn(bank[6][0:NS, KTILES * R:(KTILES + 1) * R], Ps[:, KEYS:KEYS + NS]).then_inc(*mark("sptr", b))
            pe.wait_ge(*at("spt", b))
            take(7, "satt", b)
            vs = cached[(2 * b + 1) % 3]
            pe.wait_ge(*at(f"cached{(2 * b + 1) % 3}", (2 * b + 1, OLD // P - 1)))
            for k in range(AT):
                for a in range(KTILES):
                    mm(bank[7][:, 8 * k:8 * k + 8], vs[:, a, k * P:(k + 1) * P], PTs[:, a, 8 * k:8 * k + 8], a == 0, False)
                ins = mm(bank[7][:, 8 * k:8 * k + 8], V[0:NS, TT, k * P:(k + 1) * P], PTs[0:NS, KTILES, 8 * k:8 * k + 8], False, True)
            ins.then_inc(*mark("spv", b))

        turn_keys(0)
        scores(0)
        for b in range(BD):
            if b + 1 < BD:
                turn_keys(b + 1)
            values(b)
            if b + 1 < BD:
                scores(b + 1)
        pe.wait_ge(*at("satt", BD - 1))
        take(6, "att8", 0)
        for k in range(AT):
            ins = turn(bank[6][0:NS, k * P:(k + 1) * P], attsT[:, k, :])
        ins.then_inc(*mark("att8_t", 0))

        for m in range(NT):
            take(m % 2, "mlo", m)
            for i in range(MT):
                pe.wait_ge(*at("mn", i))
                ins = turn(bank[m % 2][:, i * P:(i + 1) * P], mtk[i][:, m * P:(m + 1) * P])
            ins.then_inc(*mark("mt", m))
        pe.wait_ge(*at("mlo", NT - 1))

        def turn_mem(kind, m):
            pe.wait_ge(*at("mkv", (kind, m)))
            src = MKT if kind == "w_mk" else MVT
            take(4 + m % 2, "mtok", (kind, m))
            for i in range(MT):
                ins = turn(bank[4 + m % 2][:, i * P:(i + 1) * P], src[:, m, i * P:(i + 1) * P])
            ins.then_inc(*mark("mtk_t", (kind, m)))

        before = None
        for kind in ("w_mk", "w_mv"):
            for m in range(NT):
                u = unit_of[kind, m]
                take(2 + u % 2, "mkv", (kind, m))
                pe.wait_ge(*at("w_lo", u))
                split_product(bank[2 + u % 2][:, 0:NM], u, lambda k: mhi[:, k, :], lambda k: mlo[:, k, :]).then_inc(*mark("unit", u))
                if before:
                    turn_mem(*before)
                before = (kind, m)
        turn_mem(*before)

        n = 0
        for c in range(CH):
            cols = slice(c * CW, (c + 1) * CW)
            pe.wait_ge(*at("conv", "end"))
            take(7, "cc", (c, CT - 1))
            for k in range(CT):
                ins = mm(bank[7][:, 0:CW], ones_c[:, :], C[:, k, cols], k == 0, k == CT - 1)
            ins.then_inc(*mark("cmean", c))
            take(6, "csd", (0, c))
            for k in range(CT):
                pe.wait_ge(*at("csq", n))
                mm(bank[6][:, 0:CW], ones_c[:, :], SQ[n % 2][:, :], k == 0, k == CT - 1).then_inc(*mark("csq_used", n))
                n += 1
        for c in range(CH):
            take(6, "csd", (1, c))
            for k in range(CT):
                pe.wait_ge(*at("csq", n))
                mm(bank[6][:, 0:CW], ones_c[:, :], SQ[n % 2][:, :], k == 0, k == CT - 1).then_inc(*mark("csq_used", n))
                n += 1

        def turn_att(c):
            for m in range(AT):
                b = 4 + (c * AT + m) % 2
                take(b, "op_lo", ("mix", c, m))
                for (i, r, rows, off) in pieces(c):
                    pe.wait_ge(*at("attn", i))
                    ins = turn(bank[b][:, off:off + rows], ATT[r:r + rows, i, m * P:(m + 1) * P], r)
                ins.then_inc(*mark("att_t", (c, m)))

        sq_last = [-1]

        def means(key):
            take(6, "std", key)
            sq_last[0] += NT
            pe.wait_ge(*at("sqsum", sq_last[0]))
            mm(bank[6][:, 0:CW], ones_d[:, :], SSUM[:, :], True, True).then_inc(*mark("means", key))

        def turn_x(c):
            for k, (s, (i, r, n, off)) in enumerate(zip(XSLOT[c], pieces(c))):
                pe.wait_ge(*at(f"xtok{s}", (c, i)))
                for hf in range(2):
                    take(4 + hf, "xcp", (c, k, hf))
                    for m in range(4):
                        ins = turn(bank[4 + hf][:, m * P:m * P + n], xtok[s][r:r + n, (4 * hf + m) * P:(4 * hf + m + 1) * P], r)
                    ins.then_inc(*mark("xtr", (c, k, hf)))

        def project(name, c, m):
            u = unit_of[name, c, m]
            b = bank_of(u)
            src = {"out": "mix", "act": "ffn", "lin": "ffn"}.get(name, name)
            if name == "act":
                take(b, "aev", (c, m))
            elif name == "lin":
                take(b, "fmul", (c, m))
            else:
                take(b, "y", (name, c, m))
            s = SLOT[src, c]
            pe.wait_ge(*at("w_lo", u))
            if m == 0:
                pe.wait_ge(*at("op_lo", (src, c, NT - 1)))
                if name == "xo" and c == CH - 1:
                    pe.wait_ge(*at("op_lo", ("xo", c, "s")))
            split_product(bank[b][:, 0:CW], u, lambda k: op_hi[s][:, k, :], lambda k: op_lo[s][:, k, :]).then_inc(*mark("unit", u))

        turn_att(0)
        turn_att(1)
        for c in range(CH):
            for m in range(NT):
                project("out", c, m)
                if c > 0 and m == 1:
                    turn_x(c - 1)
                    means(("out", c - 1, "y"))
                if c > 0 and m == 3:
                    means(("out", c - 1, "x"))
                    if c == 1:
                        turn_att(2)
        after = ("out", CH - 1)
        for c in range(CH):
            for m in range(NT):
                project("xq", c, m)
                if m == 1:
                    if after[0] == "out":
                        turn_x(after[1])
                    means((*after, "y"))
                if m == 3:
                    means((*after, "x"))
            n_all = CW if c < CH - 1 else SP0
            pe.wait_ge(*at("y", ("xq", c, NT - 1)))

            def xscores(h):
                g = c * XH + h
                for t, (q0, qn) in enumerate(QTS[c]):
                    bk, o = (0, t * NM) if t < 2 else (1, 0)
                    if t != 1:
                        take(2 * (g % 2) + bk, "xexp", (g, 1 if t == 0 else 2))
                    for e in range(2):
                        ins = mm(bank[2 * (g % 2) + bk][0:qn, o:o + NM], Y[:, 2 * h + e, q0:q0 + qn], MKT[:, 2 * h + e, :], e == 0, e == 1)
                    ins.then_inc(*mark("xsc", (g, t)))

            def xvalues(h):
                g = c * XH + h
                for mt in range(MT):
                    take(4 + mt, "xpt", (g, mt))
                    for t, (q0, qn) in enumerate(QTS[c]):
                        pe.wait_ge(*at("xpn", (g, t)))
                        ins = turn(bank[4 + mt][:, q0:q0 + qn], PX[g % 2][0:qn, t, mt * P:(mt + 1) * P])
                    ins.then_inc(*mark("xptr", (g, mt)))
                for e in range(2):
                    take(6 + e, "op_lo", ("xo", c, 2 * h + e))
                    for mt in range(MT):
                        pe.wait_ge(*at("xpt", (g, mt)))
                        ins = mm(bank[6 + e][:, 0:n_all], MV[:, mt, (2 * h + e) * P:(2 * h + e + 1) * P], PTX[g % 2][:, mt, 0:n_all], mt == 0, mt == MT - 1)
                    ins.then_inc(*mark("xpv", (g, e)))

            def turn_memory(b):
                for mt in range(MT):
                    pe.wait_ge(*at(f"kmraw{b % 2}{mt}", b))
                    for hf in range(2):
                        take(2 * mt + hf, "ktm", (b, mt, hf))
                        for k in range(4):
                            ins = turn(bank[2 * mt + hf][:, k * P:(k + 1) * P], kmraw[b % 2][mt][:, (4 * hf + k) * P:(4 * hf + k + 1) * P])
                        ins.then_inc(*mark("mtr", (b, mt, hf)))

            xscores(0)
            for h in range(XH):
                if h + 1 < XH:
                    xscores(h + 1)
                xvalues(h)
            if c == CH - 1:
                turn_memory(0)
                for b in range(BD):
                    pe.wait_ge(*at("ktm", (b, MT - 1, 1)))
                    pe.wait_ge(*at("qbx", b))
                    take(4, "mexp", b)
                    for k in range(NT):
                        ins = mm(bank[4][0:16, 0:NM], qbx[b % 2][:, 16 * k:16 * k + 16], KTm[:, k, :], k == 0, k == NT - 1)
                    ins.then_inc(*mark("msc", b))
                    if b + 1 < BD:
                        turn_memory(b + 1)
                    pe.wait_ge(*at("mpn", b))
                    take(5, "mpt", b)
                    for mt in range(MT):
                        ins = turn(bank[5][:, mt * 16:(mt + 1) * 16], PX[0][0:16, 0, mt * P:(mt + 1) * P])
                    ins.then_inc(*mark("mptr", b))
                    pe.wait_ge(*at("mpt", b))
                    pe.wait_ge(*at(f"vm{b % 2}", b))
                    if b == 0:
                        take(7, "op_lo", ("xo", c, "s"))
                    for k in range(NT):
                        h = k // 2
                        for mt in range(MT):
                            ins = mm(bank[7][:, k * NS + b * TD:k * NS + (b + 1) * TD], vm[b % 2][:, mt, k * P:(k + 1) * P], PTm[:, mt, 4 * h:4 * h + 4], mt == 0, mt == MT - 1)
                    ins.then_inc(*mark("mpv", b))
            for m in range(NT):
                project("xo", c, m)
            after = ("xo", c)

        def outputs(c):
            for k, (i, r, n, off) in enumerate(pieces(c)):
                for hf in range(2):
                    g = otr[0]
                    otr[0] += 1
                    take(4 + g % 2, "ot_ev", g)
                    pe.wait_ge(*at("xfin", (c, NT - 1)))
                    for m in range(4):
                        ins = turn(bank[4 + g % 2][0:n, m * P:(m + 1) * P], XT[c][:, 4 * hf + m, off:off + n])
                    ins.then_inc(*mark("otr", g))

        otr = [0]
        for c in range(CH):
            for j in range(FT):
                project("act", c, j)
                project("lin", c, j)
                if j == 0:
                    means(("xo", CH - 1, "y") if c == 0 else ("down", c - 1, "y"))
                if j == 1:
                    if c == 0:
                        means(("xo", CH - 1, "x"))
                    else:
                        outputs(c - 1)
            for m in range(NT):
                for k0, nk in DOWN:
                    u = unit_of["down", c, m, k0]
                    if k0 == 0:
                        take(m % 4, "y", ("down", c, m))
                    pe.wait_ge(*at("w_lo", u))
                    pe.wait_ge(*at("flo", (c, min(k0 + 8, FT) - 1)))
                    last = k0 + nk == FT
                    split_product(bank[m % 4][:, 0:CW], u, lambda k: fhi[:, k0 + k, :], lambda k: flo[k0 + k], k0, k0 == 0, last).then_inc(*mark("unit", u))
        means(("down", CH - 1, "y"))
        outputs(CH - 1)
        pe.wait_ge(*at("acar", (CH - 1, FT - 1)))
        take(6, "fst", 2)
        for t in range(3):
            n = min(P, 16 * FT - t * P)
            ins = turn(bank[6][0:n, t * P:(t + 1) * P], sffn[:, :, :].rearrange("p a k -> p (a k)")[:, t * P:t * P + n])
        ins = turn(bank[6][0:2 * FT, 3 * P:4 * P], carry[:, :, :].rearrange("p a k -> p (a k)"))
        ins.then_inc(*mark("fst_t", 0))

    @block.vector
    def _(dve):
        def stt(out, in0, scalar, in1, op0, op1):
            return dve.scalar_tensor_tensor(out=out, in0=in0, scalar=scalar, in1=in1, op0=op0, op1=op1)

        def masked_max(out, scores, bias, acc, start):
            return dve.tensor_tensor_reduce(out=out, in0=scores, in1=bias, scale=SCALE, scalar=start, op0=ALU.add, op1=ALU.max, accum_out=acc)

        dve.wait_ge(*at("prm_t", 0))
        dve.tensor_copy(prm[:, :], bank[7][:, 0:PRM_N]).then_inc(*mark("prm", 0))
        dve.tensor_copy(cw[:, :, :].rearrange("p a k -> p (a k)"), bank[7][:, PRM_N:PRM_N + KW * CT]).then_inc(*mark("prm", 1))
        dve.tensor_copy(fw[:, :, :].rearrange("p a k -> p (a k)"), bank[7][:, 200:200 + 3 * FT]).then_inc(*mark("prm", 2))
        dve.wait_ge(*at("prm_t", 1))
        dve.tensor_copy(sffn[:, :, :].rearrange("p a k -> p (a k)"), bank[4][:, 0:16 * FT]).then_inc(*mark("prm", 3))
        for i in range(2):
            dve.wait_ge(*at("prm_t", 2 + i))
            for k in range(CT):
                ins = dve.tensor_copy(US[:, k, 4 * i:4 * i + 4, 0:PAD], bank[5 + i][:, k * 120:(k + 1) * 120].rearrange("p (b t) -> p b t", b=4))
                ins.then_inc(*mark("prm", "end" if (i, k) == (1, CT - 1) else (4, i, k)))
        for g in range(3):
            dve.wait_ge(*at("xss", (3 * g + 2, 1)))
            dve.tensor_tensor(rx[:, 3 * g:3 * g + 3], ssx[:, 3 * g:3 * g + 3, 0], ssx[:, 3 * g:3 * g + 3, 1], ALU.add).then_inc(*mark("xms", g))
            dve.wait_ge(*at("xsd", g))
            dve.reciprocal(rx3[:, 3 * g:3 * g + 3], rx2[:, 3 * g:3 * g + 3]).then_inc(*mark("xr", g))
            dve.wait_ge(*at("xr", g))
            for i in range(3 * g, 3 * g + 3):
                n = P if i < TT else NS
                dve.tensor_scalar(xt[i][0:n, :], xt[i][0:n, :], rx3[0:n, i:i + 1], None, ALU.mult).then_inc(*mark("xn", i))
        dve.wait_ge(*at("prm", "end"))
        n = 0
        for c in range(CH):
            for m in range(NT):
                dve.wait_ge(*at("h1hi", (c, m)))
                cols = slice(c * CW, (c + 1) * CW)
                stt(h1lo[:, m, cols], bank[4 + n % 2][:, 0:CW], g_of("g_pre_mix", m), h1hi[:, m, cols].bitcast(F32), ALU.mult, ALU.subtract).then_inc(*mark("h1lo", (c, m)))
                n += 1

        jobs = [(k, t, grp) for k in range(CT) for t in range(KW) for grp in "ps"]
        at_job = [0]

        def conv(count):
            while count and at_job[0] < len(jobs):
                k, t, grp = jobs[at_job[0]]
                at_job[0] += 1
                count -= 1
                if t == 0:
                    dve.wait_ge(*at("u", (k, "s")))
                    dve.wait_ge(*at("const", "all"))
                else:
                    dve.wait_ge(*at("conv", (k, t - 1, grp)))
                w = cw[:, t, k:k + 1]
                if grp == "p":
                    out, src = C[:, k, 0:SEQ], U[:, k, t:t + SEQ]
                else:
                    out, src = C[:, k, SEQ:NTOK].rearrange("p (b t) -> p b t", t=TD), US[:, k, :, t:t + TD]
                if t == 0:
                    ins = dve.tensor_scalar(out, src, w, g_of("conv_b", k), ALU.mult, ALU.add)
                else:
                    ins = stt(out, src, w, out, ALU.mult, ALU.add)
                ins.then_inc(*mark("conv", "end" if at_job[0] == len(jobs) else (k, t, grp)))

        def tok_kv(kind, i):
            dst = KS if kind == "k" else V
            for grp in range(3):
                dve.wait_ge(*at("ztr", (kind, i, grp)))
                if kind == "v" and i == 0 and grp == 0:
                    dve.wait_ge(*at("ks_out", TT))
                if grp < 2:
                    ins = dve.tensor_copy(dst[:, 4 * grp:4 * grp + 4, i * P:(i + 1) * P], bank[6 + grp][:, :].rearrange("p (t n) -> p t n", t=4))
                else:
                    ins = dve.tensor_copy(dst[0:NS, TT, i * P:(i + 1) * P], bank[6][0:NS, 0:P])
                ins.then_inc(*mark("ztok", (kind, i, grp)))

        before = None
        for kind, i, _ in order_in:
            u = unit_of[kind, i]
            if kind == "a":
                for c in range(CH):
                    need_uc(dve, u, c)
                    b = bank[3 * (u % 2) + c]
                    n = SP0 if c == CH - 1 else CW
                    cols = U[:, i, PAD + c * CW:PAD + c * CW + n]
                    dve.wait_ge(*at("sig", (i, c)))
                    dve.tensor_tensor(cols, b[:, 0:n], cols, ALU.mult).then_inc(*mark("u", (i, c)))
                    if c == CH - 1:
                        dve.wait_ge(*at("sig", (i, "s")))
                        cols = US[:, i, :, PAD:]
                        dve.tensor_tensor(cols, b[:, SP0:CW].rearrange("p (b t) -> p b t", t=TD), cols, ALU.mult).then_inc(*mark("u", (i, "s")))
            if before and before[0] in ("k", "v"):
                tok_kv(*before)
            if kind in ("k", "v", "q"):
                conv(14)
            before = (kind, i)

        dve.wait_ge(*at("tables", "s"))
        for s in range(len(STEPS) + 2):
            if s < len(STEPS):
                i, h = STEPS[s]
                q, n = s % 2, (i + 1) * P
                dve.wait_ge(*at("score", s))
                if s >= 2:
                    dve.wait_ge(*at("ptr", s - 2))
                else:
                    dve.wait_ge(*at("unit", FIRST_MEM - 1))
                parts = -(-n // 512)
                for part in range(parts):
                    k0, k1 = part * 512, min(n, part * 512 + 512)
                    w0 = (TT - 1 - i) * P + k0
                    if part:
                        dve.wait_ge(*at("pm", (s, 0)))
                    masked_max(Pp[q][:, k0:k1], bank[2 * q + part][:, 0:k1 - k0], wt[:, w0:w0 + k1 - k0], mx[:, q, part:part + 1],
                                    mx[:, q, 0:1] if part else -3e38).then_inc(*mark("pm", (s, part)))
                dve.wait_ge(*at("pm", (s, parts - 1)))
                dve.tensor_scalar(negm[:, q:q + 1], mx[:, q, parts - 1:parts], -1.0, None, ALU.mult).then_inc(*mark("pmax", s))
            if 1 <= s <= len(STEPS):
                q = (s - 1) % 2
                dve.wait_ge(*at("pexp", s - 1))
                if s >= 3:
                    dve.wait_ge(*at("att", s - 3))
                dve.reciprocal(rden[:, q:q + 1], den[:, q:q + 1]).then_inc(*mark("prd", s - 1))
            if s >= 2:
                i, h = STEPS[s - 2]
                q = s % 2
                dve.wait_ge(*at("pv", s - 2))
                dve.wait_ge(*at("prd", s - 2))
                dve.tensor_scalar(ATT[:, i, h * DH:(h + 1) * DH], bank[6 + q][:, 0:DH], rden[:, q:q + 1], None, ALU.mult).then_inc(*mark("att", s - 2))
            conv(2)
        dve.tensor_copy(usn[:, :, :].rearrange("p k (b t) -> p k b t", t=TD), US[:, :, :, PAD:]).then_inc(*mark("usn", 0))
        conv(len(jobs))
        for k, n in ((0, PAD), (1, NS)):
            dve.wait_ge(*at("cst_t", k))
            dve.tensor_copy(cst[0:n, k, :], bank[6 + k][0:n, :]).then_inc(*mark("cst", k))

        R = H * TD

        def spread_queries(b):
            if b >= 2:
                dve.wait_ge(*at("ssc", b - 2))
            dve.wait_ge(*at("zt", ("q", AT - 1, CH - 1)))
            v = qbd[b % 2][:, :].rearrange("p (k x) -> p k x", x=40)
            cols = slice(SEQ + b * TD, SEQ + (b + 1) * TD)
            dve.tensor_copy(v[0:64, :, 0:4], QT[0:64, :, cols]).then_inc(*mark("qbd_a", b))
            dve.tensor_copy(v[64:128, :, 4:8], QT[64:128, :, cols]).then_inc(*mark("qbd", b))

        spread_queries(0)
        for b in range(BD):
            if b + 1 < BD:
                spread_queries(b + 1)
            dve.wait_ge(*at("ssc", b))
            if b > 0:
                dve.wait_ge(*at("sptr", b - 1))
            parts = ((0, 512, bank[4][0:R, 0:512], ws[:, 0:512]), (512, KEYS, bank[5][0:R, 0:KEYS - 512], ws[:, 512:KEYS]),
                     (KEYS, KEYS + NS, bank[5][0:R, KEYS - 512:KEYS - 512 + NS], ws[:, KEYS + b * NS:KEYS + (b + 1) * NS]))
            for k, (k0, k1, src, bias) in enumerate(parts):
                if k:
                    dve.wait_ge(*at("sm", (b, k - 1)))
                masked_max(Ps[:, k0:k1], src, bias, mx[0:R, 0, k:k + 1], mx[0:R, 0, k - 1:k] if k else -3e38).then_inc(*mark("sm", (b, k)))
            dve.wait_ge(*at("sm", (b, 2)))
            dve.tensor_scalar(negm[0:R, 2:3], mx[0:R, 0, 2:3], -1.0, None, ALU.mult).then_inc(*mark("smax", b))
            dve.wait_ge(*at("sexp", b))
            dve.reciprocal(rden[0:R, 2:3], den[0:R, 2:3]).then_inc(*mark("srd", b))
            dve.wait_ge(*at("srd", b))
            dve.tensor_scalar(Ps[:, :], Ps[:, :], rden[0:R, 2:3], None, ALU.mult).then_inc(*mark("spn", b))
            dve.wait_ge(*at("sptr", b))
            dve.tensor_copy(PTs[:, 0:KTILES, :], bank[6][:, 0:KTILES * R].rearrange("p (a n) -> p a n", n=R)).then_inc(*mark("spt_a", b))
            dve.tensor_copy(PTs[0:NS, KTILES, :], bank[6][0:NS, KTILES * R:(KTILES + 1) * R]).then_inc(*mark("spt", b))
            dve.wait_ge(*at("spv", b))
            v = bank[7][:, 0:AT * 8].rearrange("p (k x) -> p k x", x=8)
            cols = slice(b * TD, (b + 1) * TD)
            dve.tensor_copy(attsT[0:64, :, cols], v[0:64, :, 0:4]).then_inc(*mark("satt_a", b))
            dve.tensor_copy(attsT[64:128, :, cols], v[64:128, :, 4:8]).then_inc(*mark("satt", b))
        dve.wait_ge(*at("att8_t", 0))
        dve.tensor_copy(ATT[0:NS, TT, :], bank[6][0:NS, :]).then_inc(*mark("att8", 0))
        dve.wait_ge(*at("ass", TT))
        dve.tensor_scalar(rx[:, 0:9], ssx[:, 0:9, 0], 1.0 / AW, None, ALU.mult).then_inc(*mark("ams_a", 0))
        dve.tensor_tensor(rx[:, 9:11], ssx[:, 9:11, 0], ssx[:, 9:11, 1], ALU.add).then_inc(*mark("ams_a", 1))
        dve.wait_ge(*at("ams_a", 1))
        dve.tensor_scalar(rx[:, 9:11], rx[:, 9:11], 1.0 / D, None, ALU.mult).then_inc(*mark("ams", 0))
        dve.wait_ge(*at("asd", 0))
        dve.reciprocal(rx3[:, 0:11], rx2[:, 0:11]).then_inc(*mark("ar", 0))
        dve.wait_ge(*at("ar", 0))
        for i in range(MT):
            dve.tensor_scalar(mtk[i][:, :], mtk[i][:, :], rx3[:, 9 + i:10 + i], None, ALU.mult).then_inc(*mark("mn", i))
        for i in range(TT + 1):
            n = P if i < TT else NS
            dve.tensor_scalar(ATT[0:n, i, :], ATT[0:n, i, :], rx3[0:n, i:i + 1], None, ALU.mult).then_inc(*mark("attn", i))
        for m in range(NT):
            dve.wait_ge(*at("mhi", m))
            stt(mlo[:, m, :], bank[m % 2][:, 0:NM], g_of("g_mem", m), mhi[:, m, :].bitcast(F32), ALU.mult, ALU.subtract).then_inc(*mark("mlo", m))
        dve.wait_ge(*at("v_out", TT))
        for kind in ("w_mk", "w_mv"):
            for m in range(NT):
                dve.wait_ge(*at("mtk_t", (kind, m)))
                if kind == "w_mv" and m == 0:
                    dve.wait_ge(*at("cst_t", 1))
                dve.tensor_copy((MKO if kind == "w_mk" else MV)[:, :, m * P:(m + 1) * P],
                                     bank[4 + m % 2][:, 0:NM].rearrange("p (t n) -> p t n", t=MT)).then_inc(*mark("mtok", (kind, m)))

        for c in range(CH):
            cols = slice(c * CW, (c + 1) * CW)
            dve.wait_ge(*at("cmean", c))
            for k in range(CT):
                dve.tensor_tensor(C[:, k, cols], C[:, k, cols], bank[7][:, 0:CW], ALU.subtract).then_inc(*mark("cc", (c, k)))
        for c in range(CH):
            cols = slice(c * CW, (c + 1) * CW)
            dve.wait_ge(*at("csd", (0, c)))
            dve.reciprocal(RSC[:, c, :], STD[:, :]).then_inc(*mark("crs", (0, c)))
            dve.wait_ge(*at("crs", (0, c)))
            for k in range(CT):
                dve.tensor_tensor(C[:, k, cols], C[:, k, cols], RSC[:, c, :], ALU.mult).then_inc(*mark("cn", (c, k)))
        for c in range(CH):
            cols = slice(c * CW, (c + 1) * CW)
            dve.wait_ge(*at("csd", (1, c)))
            dve.reciprocal(RSC[:, c, :], STD[:, :]).then_inc(*mark("crs", (1, c)))
            dve.wait_ge(*at("crs", (1, c)))
            for k in range(CT):
                dve.tensor_tensor(C[:, k, cols], C[:, k, cols], RSC[:, c, :], ALU.mult).then_inc(*mark("cf", (c, k)))

        def mix(c):
            s = SLOT["mix", c]
            for m in range(AT):
                dve.wait_ge(*at("op_hi", ("mix", c, m)))
                stt(op_lo[s][:, m, :], bank[4 + (c * AT + m) % 2][:, 0:CW], g_of("g_out_attn", m), op_hi[s][:, m, :].bitcast(F32), ALU.mult, ALU.subtract).then_inc(*mark("op_lo", ("mix", c, m)))
            for m in range(CT):
                dve.wait_ge(*at("op_hi", ("mix", c, AT + m)))
                stt(op_lo[s][:, AT + m, :], C[:, m, c * CW:(c + 1) * CW], g_of("g_out_conv", m), op_hi[s][:, AT + m, :].bitcast(F32), ALU.mult, ALU.subtract).then_inc(*mark("op_lo", ("mix", c, AT + m)))

        sums = [0]
        ox_low = [None, None]
        last_means = [None]

        def add_square(sq):
            n = sums[0]
            dve.wait_ge(*at("sq", n))
            if n % NT == 0:
                if last_means[0]:
                    dve.wait_ge(*at("means", last_means[0]))
                ins = dve.tensor_copy(SSUM[:, :], sq[n % 2][:, :])
            else:
                dve.wait_ge(*at("sqsum", n - 1))
                ins = dve.tensor_tensor(SSUM[:, :], SSUM[:, :], sq[n % 2][:, :], ALU.add)
            ins.then_inc(*mark("sqsum", n))
            sums[0] += 1

        def inverse_root(key, out):
            dve.wait_ge(*at("std", key))
            dve.reciprocal(out, STD[:, :]).then_inc(*mark("rstd", key))
            dve.wait_ge(*at("rstd", key))
            last_means[0] = key

        def scaled_y(name, c, m):
            stt(Y[:, m, :], Y[:, m, :], g_of(POST[name], m), RSTD[:, :], ALU.mult, ALU.mult).then_inc(*mark("yn", (name, c, m)))
            dve.wait_ge(*at("yn", (name, c, m)))

        def update(name, c):
            inverse_root((name, c, "y"), RSTD[:, :])
            if name == "out":
                dve.wait_ge(*at("xcp", (c, len(pieces(c)) - 1, 1)))
            for m in range(NT):
                scaled_y(name, c, m)
                dve.tensor_tensor(XT[c][:, m, :], XT[c][:, m, :], Y[:, m, :], ALU.add).then_inc(*mark("x", (name, c, m)))
                if m:
                    add_square(SQ)
            add_square(SQ)
            inverse_root((name, c, "x"), RSX[:, c, :])

        def operand(name, c):
            s = SLOT[name, c]
            dve.wait_ge(*at("unit", unit_of[FREE[name, c]]))

            def low(m):
                dve.wait_ge(*at("op_hi", (name, c, m)))
                stt(op_lo[s][:, m, :], OX[m % 2][:, :], g_of(GAIN[name], m), op_hi[s][:, m, :].bitcast(F32), ALU.mult, ALU.subtract).then_inc(*mark("op_lo", (name, c, m)))

            for m in range(NT):
                if m >= 2:
                    dve.wait_ge(*at("op_lo", (name, c, m - 2)))
                elif ox_low[m]:
                    dve.wait_ge(*at("op_lo", ox_low[m]))
                ox_low[m % 2] = (name, c, m)
                dve.tensor_tensor(OX[m % 2][:, :], XT[c][:, m, :], RSX[:, c, :], ALU.mult).then_inc(*mark("opx", (name, c, m)))
                if m:
                    low(m - 1)
            low(NT - 1)

        mix(0)
        mix(1)
        for c in range(CH):
            for m in range(NT):
                add_square(SQ)
            update("out", c)
            if c == 0:
                mix(2)
            if c == 1:
                operand("xq", 0)
        for c in range(CH):
            n_all = CW if c < CH - 1 else SP0
            for h in range(XH):
                g = c * XH + h
                for t, (q0, qn) in enumerate(QTS[c]):
                    bk, o = (0, t * NM) if t < 2 else (1, 0)
                    dve.wait_ge(*at("xsc", (g, max(t, 1))))
                    if g:
                        dve.wait_ge(*at("xexp", (g - 1, t)))
                    dve.tensor_reduce(mx[0:qn, 0, t:t + 1], bank[2 * (g % 2) + bk][0:qn, o:o + NM], AX.X, ALU.max).then_inc(*mark("xm", (g, t)))
                    dve.wait_ge(*at("xm", (g, t)))
                    dve.tensor_scalar(negm[0:qn, t:t + 1], mx[0:qn, 0, t:t + 1], -XSCALE, None, ALU.mult).then_inc(*mark("xmax", (g, t)))
                for t, (q0, qn) in enumerate(QTS[c]):
                    dve.wait_ge(*at("xexp", (g, t)))
                    dve.reciprocal(rden[0:qn, t:t + 1], den[0:qn, t:t + 1]).then_inc(*mark("xrd", (g, t)))
                    dve.wait_ge(*at("xrd", (g, t)))
                    dve.tensor_scalar(PX[g % 2][0:qn, t, :], PX[g % 2][0:qn, t, :], rden[0:qn, t:t + 1], None, ALU.mult).then_inc(*mark("xpn", (g, t)))
                for e in range(2):
                    k = 2 * h + e
                    dve.wait_ge(*at("op_hi", ("xo", c, k)))
                    dve.tensor_tensor(op_lo[0][:, k, 0:n_all], bank[6 + e][:, 0:n_all], op_hi[0][:, k, 0:n_all].bitcast(F32), ALU.subtract).then_inc(*mark("op_lo", ("xo", c, k)))
            if c == CH - 1:
                for b in range(BD):
                    if b >= 2:
                        dve.wait_ge(*at("msc", b - 2))
                    v = qbx[b % 2][:, :].rearrange("p (h x) -> p h x", x=36)
                    src = Y[:, :, SP0 + b * TD:SP0 + (b + 1) * TD].rearrange("p (h e) t -> p h e t", e=2)
                    dve.tensor_copy(v[:, :, 0:4], src[:, :, 0, :]).then_inc(*mark("qbx_a", b))
                    dve.tensor_copy(v[:, :, 16:20], src[:, :, 1, :]).then_inc(*mark("qbx", b))
                    dve.wait_ge(*at("msc", b))
                    dve.tensor_reduce(mx[0:16, 1, 0:1], bank[4][0:16, 0:NM], AX.X, ALU.max).then_inc(*mark("mm", b))
                    dve.wait_ge(*at("mm", b))
                    dve.tensor_scalar(negm[0:16, 3:4], mx[0:16, 1, 0:1], -XSCALE, None, ALU.mult).then_inc(*mark("mmax", b))
                    dve.wait_ge(*at("mexp", b))
                    dve.reciprocal(rden[0:16, 3:4], den[0:16, 3:4]).then_inc(*mark("mrd", b))
                    dve.wait_ge(*at("mrd", b))
                    dve.tensor_scalar(PX[0][0:16, 0, :], PX[0][0:16, 0, :], rden[0:16, 3:4], None, ALU.mult).then_inc(*mark("mpn", b))
                    dve.wait_ge(*at("mptr", b))
                    dve.tensor_copy(PTm[:, :, :], bank[5][:, 0:2 * 16].rearrange("p (t n) -> p t n", t=2)).then_inc(*mark("mpt", b))
                dve.wait_ge(*at("op_hi", ("xo", c, "s")))
                dve.tensor_tensor(op_lo[0][:, :, SP0:CW], bank[7][:, 0:NT * NS].rearrange("p (k n) -> p k n", k=NT),
                                       op_hi[0][:, :, SP0:CW].bitcast(F32), ALU.subtract).then_inc(*mark("op_lo", ("xo", c, "s")))
            if c < CH - 1:
                operand("xq", c + 1)
            else:
                operand("ffn", 0)
            for m in range(NT):
                add_square(SQ)
            update("xo", c)
        operand("ffn", 1)

        for c in range(CH):
            for j in range(FT):
                a, o = aext[j % 2], cv[j % 2]
                n = CW if c < CH - 1 else SP0
                sa = a[:, 2 + SP0:2 + SP0 + 48].rearrange("p (b t) -> p b t", t=6)
                so = o[:, SP0:CW].rearrange("p (b t) -> p b t", t=TD)
                if c == 0 and j < 2:
                    dve.wait_ge(*at("op_lo", ("ffn", 1, NT - 1)))
                if j < 2 and c > 0:
                    dve.wait_ge(*at("std", ("down", c - 1, "y")))
                    if c == 1:
                        dve.wait_ge(*at("op_lo", ("ffn", 2, NT - 1)))
                if j >= 2:
                    dve.wait_ge(*at("acar", (c, j - 2)))
                ins = dve.tensor_copy(a[:, 0:2], carry[:, :, j])
                if c == CH - 1:
                    ins.then_inc(*mark("actx_p", (c, j)))
                    ins = dve.tensor_copy(sa[:, :, 0:2], sffn[:, :, j].rearrange("p (b t) -> p b t", t=2))
                ins.then_inc(*mark("actx", (c, j)))
                dve.wait_ge(*at("actx", (c, j)))
                dve.wait_ge(*at("aev", (c, j)))
                for t in range(3):
                    w = fw[:, t, j:j + 1]
                    parts = [("p", o[:, 0:n], a[:, t:t + n])] + ([("s", so, sa[:, :, t:t + TD])] if c == CH - 1 else [])
                    for grp, out, src in parts:
                        if t:
                            dve.wait_ge(*at("cvs" if grp == "s" else ("cv" if c < CH - 1 else "cvp"), (c, j, t - 1)))
                        ins = (dve.tensor_scalar(out, src, w, None, ALU.mult) if t == 0 else stt(out, src, w, out, ALU.mult, ALU.add))
                        if c < CH - 1:
                            ins.then_inc(*mark("cv", (c, j, t)))
                        elif grp == "p":
                            ins.then_inc(*mark("cvp", (c, j, t)))
                        elif t < 2:
                            ins.then_inc(*mark("cvs", (c, j, t)))
                        else:
                            ins.then_inc(*mark("cv", (c, j, t)))
                ins = dve.tensor_copy(carry[:, :, j], a[:, n:n + 2])
                if c == CH - 1:
                    ins.then_inc(*mark("acar_p", (c, j)))
                    ins = dve.tensor_copy(sffn[:, :, j].rearrange("p (b t) -> p b t", t=2), sa[:, :, 4:6])
                ins.then_inc(*mark("acar", (c, j)))
                dve.wait_ge(*at("gelu", (c, j)))
                u = unit_of["lin", c, j]
                dve.wait_ge(*at("unit", u))
                dve.tensor_tensor(o[:, :], bank[bank_of(u)][:, 0:CW], o[:, :], ALU.mult).then_inc(*mark("fmul", (c, j)))
                dve.wait_ge(*at("fhi", (c, j)))
                dve.wait_ge(*at("fmul", (c, j)))
                dve.tensor_tensor(flo[j], o[:, :], fhi[:, j, :].bitcast(F32), ALU.subtract).then_inc(*mark("flo", (c, j)))
            for m in range(NT):
                add_square(SQf)
            inverse_root(("down", c, "y"), RSTD[:, :])
            for m in range(NT):
                scaled_y("down", c, m)
                dve.tensor_tensor(XT[c][:, m, :], XT[c][:, m, :], Y[:, m, :], ALU.add).then_inc(*mark("xfin", (c, m)))
            if c == 0:
                operand("ffn", 2)
        dve.wait_ge(*at("fst_t", 0))
        dve.wait_ge(*at("xfin", (CH - 1, NT - 1)))
        for t in (3, 0, 1, 2):
            n = 2 * FT if t == 3 else min(P, 16 * FT - t * P)
            dve.tensor_copy(fst[0:n, t, :], bank[6][0:n, t * P:(t + 1) * P]).then_inc(*mark("fst", t))

    return S


_INS = ["x_prompt", "x_sample", "mem_prompt", "cache_win_k", "cache_win_v", "state_conv", "state_ffn_conv",
        "cache_mem_k", "cache_mem_v", "g_pre_mix", "w_in", "conv_w", "conv_b", "ln_conv_g", "ln_conv_b",
        "g_out_attn", "g_out_conv", "w_out", "g_post_mix", "g_pre_x", "g_mem", "w_xq", "w_mk", "w_mv", "w_xo",
        "g_post_x", "g_pre_ffn", "w_up", "ffn_conv_w", "w_down", "g_post_ffn"]
_OUTS = [("y_p", (1, SEQ, D)), ("y_s", (BD, TD, D)), ("win_k_p", (1, 1, SEQ, H, DH)), ("win_v_p", (1, 1, SEQ, H, DH)),
         ("conv_p", (1, 1, PAD, CC)), ("ffn_p", (1, 1, 2, DF)), ("mem_k", (1, 1, NM, XH, XD)), ("mem_v", (1, 1, NM, XH, XD)),
         ("win_k_s", (1, BD, TD, H, DH)), ("win_v_s", (1, BD, TD, H, DH)), ("conv_s", (1, BD, PAD, CC)), ("ffn_s", (1, BD, 2, DF))]


def constants():
    return {"identity": np.eye(P, dtype=np.float32), "prompt_bias": prompt_bias(), "sample_bias": sample_bias()}


def build(nc, shapes, counts):
    A = {n: nc.dram_tensor(f"in_{n}_dram", shape, F32, kind="ExternalInput").ap() for n, shape in shapes.items()}
    O = {n: nc.dram_tensor(f"out_{i}_dram", shape, F32, kind="ExternalOutput").ap() for i, (n, shape) in enumerate(_OUTS)}
    with ExitStack() as ctx:
        return layout(nc, ctx, A, O, counts)


def kernel(**inputs):
    import concourse.bacc as _bacc
    from concourse.bass_utils import run_bass_kernel_spmd as _run

    arrays = {n: np.ascontiguousarray(inputs[n]) for n in _INS}
    arrays.update(constants())
    shapes = {n: a.shape for n, a in arrays.items()}
    counts = build(_bacc.Bacc("TRN2", target_bir_lowering=False, num_devices=1), shapes, None).noted
    nc = _bacc.Bacc("TRN2", target_bir_lowering=False, num_devices=1)
    build(nc, shapes, counts)
    r = _run(nc, [{f"in_{n}_dram": a for n, a in arrays.items()}], core_ids=[0])
    return tuple(r.results[0][f"out_{i}_dram"] for i in range(len(_OUTS)))
```
